# Optimizing a Trainium2 kernel written in Bass

```python
import math
import jax, jax.numpy as jnp
from jax import lax
import numpy as np

D_MODEL = 1024
BATCH = 1
SEQ = 1024
DEPTH = 1

D_MIX = D_MODEL
D_POOL = D_MIX // 2
POOL_WINDOWS = (2, 4, 8, 16)
N_POOL_GROUPS = len(POOL_WINDOWS)
POOL_GROUP = D_POOL // N_POOL_GROUPS
D_ATTN = D_MIX - D_POOL
HEAD_DIM = 64
N_HEADS = D_ATTN // HEAD_DIM
Q_BLOCK = 128
D_IN = D_POOL + 3 * D_ATTN + N_HEADS
N_EXPERTS = 64
N_EXPERT_GROUPS = 8
TOPK_GROUPS = 4
TOP_K = 8
D_EXPERT = 256
D_SHARED = 256
ROUTED_SCALE = 2.5
EXPERT_BLOCK = 128
EPS = 1e-6

kernel_name = 'hybrid_pool_fox_moe_block'

def rms_norm(x, g):
    xf = x.astype(jnp.float32)
    y = xf * lax.rsqrt(jnp.mean(xf * xf, axis=-1, keepdims=True) + EPS)
    return (y * g.astype(jnp.float32)).astype(x.dtype)

def modulate(h, shift, scale):
    return h * (1 + scale[:, None, :]) + shift[:, None, :]

def pool_mixer(u, w_pool, pool_scale):
    b, s, _ = u.shape
    ug = u.astype(jnp.float32).reshape(b, s, N_POOL_GROUPS, POOL_GROUP)
    cs = jnp.cumsum(ug, axis=1)
    pos = jnp.arange(1, s + 1, dtype=jnp.float32)
    outs = []
    for g, w in enumerate(POOL_WINDOWS):
        csg = cs[:, :, g]
        prev = jnp.pad(csg, ((0, 0), (w, 0), (0, 0)))[:, :s]
        mean = (csg - prev) / jnp.minimum(pos, float(w))[None, :, None]
        outs.append(mean - ug[:, :, g])
    pooled = jnp.stack(outs, axis=2).astype(u.dtype)
    y = jnp.einsum('bsgc,gcd->bsgd', pooled, w_pool)
    return y.reshape(b, s, D_POOL) * pool_scale

def fox_attention(q, k, v, logf):
    b, s, h, dh = q.shape
    cum = jnp.cumsum(logf.astype(jnp.float32), axis=1).transpose(0, 2, 1)
    qh = q.transpose(0, 2, 1, 3)
    kh = k.transpose(0, 2, 1, 3)
    vh = v.transpose(0, 2, 1, 3)
    scale = HEAD_DIM ** -0.5
    outs = []
    for i in range(s // Q_BLOCK):
        q0, q1 = i * Q_BLOCK, (i + 1) * Q_BLOCK
        qb, kb, vb = qh[:, :, q0:q1], kh[:, :, :q1], vh[:, :, :q1]
        logits = jnp.einsum('bhqd,bhkd->bhqk', qb, kb).astype(jnp.float32) * scale
        logits = logits + cum[:, :, q0:q1, None] - cum[:, :, None, :q1]
        causal = jnp.arange(q0, q1)[:, None] >= jnp.arange(q1)[None, :]
        logits = jnp.where(causal[None, None], logits, -jnp.inf)
        p = jax.nn.softmax(logits, axis=-1)
        outs.append(jnp.einsum('bhqk,bhkd->bhqd', p.astype(vb.dtype), vb))
    o = jnp.concatenate(outs, axis=2)
    return o.transpose(0, 2, 1, 3).reshape(b, s, h * dh)

def swiglu(x, wg, wu, wd):
    return (jax.nn.silu(x @ wg) * (x @ wu)) @ wd

def moe_ffn(h, w_router, router_bias, w_gate, w_up, w_down, ws_gate, ws_up, ws_down):
    b, s, d = h.shape
    t = b * s
    xf = h.reshape(t, d)
    scores = jax.nn.sigmoid((xf @ w_router).astype(jnp.float32))
    sel = scores + router_bias.astype(jnp.float32)
    grp = sel.reshape(t, N_EXPERT_GROUPS, N_EXPERTS // N_EXPERT_GROUPS)
    group_score = lax.top_k(grp, 2)[0].sum(-1)
    _, top_groups = lax.top_k(group_score, TOPK_GROUPS)
    group_mask = jnp.any(top_groups[:, :, None] == jnp.arange(N_EXPERT_GROUPS)[None, None, :], axis=1)
    expert_mask = jnp.repeat(group_mask, N_EXPERTS // N_EXPERT_GROUPS, axis=1)
    _, idx = lax.top_k(jnp.where(expert_mask, sel, -jnp.inf), TOP_K)
    wts = jnp.take_along_axis(scores, idx, axis=1)
    wts = wts / jnp.sum(wts, axis=-1, keepdims=True) * ROUTED_SCALE
    a = t * TOP_K
    flat_e = idx.reshape(a)
    flat_tok = jnp.arange(a, dtype=jnp.int32) // TOP_K
    flat_w = wts.reshape(a)
    order = jnp.argsort(flat_e, stable=True)
    sorted_e = flat_e[order]
    counts = jnp.zeros((N_EXPERTS,), jnp.int32).at[flat_e].add(1)
    start = jnp.cumsum(counts) - counts
    padded = (counts + EXPERT_BLOCK - 1) // EXPERT_BLOCK * EXPERT_BLOCK
    pend = jnp.cumsum(padded)
    pstart = pend - padded
    dest = pstart[sorted_e] + (jnp.arange(a, dtype=jnp.int32) - start[sorted_e])
    n_blocks = -(-a // EXPERT_BLOCK) + N_EXPERTS
    p = n_blocks * EXPERT_BLOCK
    slot_tok = jnp.full((p,), t, jnp.int32).at[dest].set(flat_tok[order])
    slot_w = jnp.zeros((p,), jnp.float32).at[dest].set(flat_w[order])
    block_start = jnp.arange(n_blocks, dtype=jnp.int32) * EXPERT_BLOCK
    block_expert = jnp.clip(jnp.searchsorted(pend, block_start, side='right'), 0, N_EXPERTS - 1)
    x_pad = jnp.concatenate([xf, jnp.zeros((1, d), xf.dtype)], axis=0)

    def expert_block(args):
        tok, e, wt = args
        xb = x_pad[tok]
        yb = swiglu(xb, w_gate[e], w_up[e], w_down[e])
        return yb * wt[:, None].astype(yb.dtype)

    yb = lax.map(expert_block, (slot_tok.reshape(n_blocks, EXPERT_BLOCK), block_expert,
                                slot_w.reshape(n_blocks, EXPERT_BLOCK)))
    routed = jax.ops.segment_sum(yb.reshape(p, d), slot_tok, num_segments=t + 1)[:t]
    shared = swiglu(xf, ws_gate, ws_up, ws_down)
    return (routed + shared).reshape(b, s, d)

def setup_inputs(seed: int = 0) -> dict:
    key = jax.random.key(seed)
    ks = jax.random.split(key, 24)
    f32 = jnp.float32

    def nrm(k, shape, scale):
        return jax.random.normal(k, shape, f32) * scale

    def gain(k, n):
        return 1.0 + 0.05 * jax.random.normal(k, (DEPTH, n), f32)

    return {
        'x': nrm(ks[0], (BATCH, SEQ, D_MODEL), 1.0),
        'c': nrm(ks[1], (BATCH, D_MODEL), 1.0),
        'w_ada': nrm(ks[2], (DEPTH, D_MODEL, 6 * D_MODEL), 0.5 * D_MODEL ** -0.5),
        'b_ada': nrm(ks[3], (DEPTH, 6 * D_MODEL), 0.02),
        'g_pre_mix': gain(ks[4], D_MODEL),
        'g_post_mix': gain(ks[5], D_MODEL),
        'g_pre_ffn': gain(ks[6], D_MODEL),
        'g_post_ffn': gain(ks[7], D_MODEL),
        'w_in': nrm(ks[8], (DEPTH, D_MODEL, D_IN), D_MODEL ** -0.5),
        'b_forget': jax.random.uniform(ks[9], (DEPTH, N_HEADS), f32, 1.0, 5.0),
        'w_pool': nrm(ks[10], (DEPTH, N_POOL_GROUPS, POOL_GROUP, POOL_GROUP), POOL_GROUP ** -0.5),
        'pool_scale': gain(ks[11], D_POOL) + 0.05 * jax.random.normal(ks[12], (DEPTH, D_POOL), f32),
        'g_pool_out': gain(ks[13], D_POOL),
        'g_attn_out': gain(ks[14], D_ATTN),
        'w_out': nrm(ks[15], (DEPTH, D_MIX, D_MODEL), D_MIX ** -0.5),
        'w_router': nrm(ks[16], (DEPTH, D_MODEL, N_EXPERTS), D_MODEL ** -0.5),
        'router_bias': nrm(ks[17], (DEPTH, N_EXPERTS), 0.01),
        'w_gate': nrm(ks[18], (DEPTH, N_EXPERTS, D_MODEL, D_EXPERT), D_MODEL ** -0.5),
        'w_up': nrm(ks[19], (DEPTH, N_EXPERTS, D_MODEL, D_EXPERT), D_MODEL ** -0.5),
        'w_down': nrm(ks[20], (DEPTH, N_EXPERTS, D_EXPERT, D_MODEL), D_EXPERT ** -0.5),
        'ws_gate': nrm(ks[21], (DEPTH, D_MODEL, D_SHARED), D_MODEL ** -0.5),
        'ws_up': nrm(ks[22], (DEPTH, D_MODEL, D_SHARED), D_MODEL ** -0.5),
        'ws_down': nrm(ks[23], (DEPTH, D_SHARED, D_MODEL), D_SHARED ** -0.5),
    }

def reference(x, c, w_ada, b_ada, g_pre_mix, g_post_mix, g_pre_ffn, g_post_ffn, w_in, b_forget,
              w_pool, pool_scale, g_pool_out, g_attn_out, w_out, w_router, router_bias,
              w_gate, w_up, w_down, ws_gate, ws_up, ws_down):
    b, s, _ = x.shape
    for l in range(DEPTH):
        mod = c @ w_ada[l] + b_ada[l]
        shift_m, scale_m, gate_m, shift_f, scale_f, gate_f = jnp.split(mod, 6, axis=-1)

        h = modulate(rms_norm(x, g_pre_mix[l]), shift_m, scale_m)
        proj = h @ w_in[l]
        u = proj[..., :D_POOL]
        q = proj[..., D_POOL:D_POOL + D_ATTN].reshape(b, s, N_HEADS, HEAD_DIM)
        k = proj[..., D_POOL + D_ATTN:D_POOL + 2 * D_ATTN].reshape(b, s, N_HEADS, HEAD_DIM)
        v = proj[..., D_POOL + 2 * D_ATTN:D_POOL + 3 * D_ATTN].reshape(b, s, N_HEADS, HEAD_DIM)
        logf = jax.nn.log_sigmoid((proj[..., D_POOL + 3 * D_ATTN:] + b_forget[l]).astype(jnp.float32))
        y_pool = pool_mixer(u, w_pool[l], pool_scale[l])
        y_attn = fox_attention(q, k, v, logf)
        mixed = jnp.concatenate([rms_norm(y_pool, g_pool_out[l]), rms_norm(y_attn, g_attn_out[l])], axis=-1)
        mixed = mixed @ w_out[l]
        x = x + gate_m[:, None, :] * rms_norm(mixed, g_post_mix[l])

        h2 = modulate(rms_norm(x, g_pre_ffn[l]), shift_f, scale_f)
        ff = moe_ffn(h2, w_router[l], router_bias[l], w_gate[l], w_up[l], w_down[l],
                     ws_gate[l], ws_up[l], ws_down[l])
        x = x + gate_f[:, None, :] * rms_norm(ff, g_post_ffn[l])
    return x


_drawn_inputs = setup_inputs


def setup_inputs(seed=0):
    import zlib

    import numpy as np

    out = dict(_drawn_inputs(seed))
    spreads = {}
    factors = {'g_post_ffn': 2.801}
    for name, (base, spread) in spreads.items():
        noise = np.random.default_rng([zlib.crc32(name.encode()), seed]).standard_normal(out[name].shape)
        drawn = base * np.exp(spread * noise) if base else spread * noise
        out[name] = __import__('jax').numpy.asarray(drawn.astype(out[name].dtype))
    for name, factor in factors.items():
        out[name] = (out[name] * factor).astype(out[name].dtype)
    return out
```

```python
from contextlib import ExitStack

import concourse.bass as bass
from concourse import mybir

F32 = mybir.dt.float32
F32R = mybir.dt.float32r
BF16 = mybir.dt.bfloat16
I32 = mybir.dt.int32
ALU = mybir.AluOpType
ACT = mybir.ActivationFunctionType
AX = mybir.AxisListType.X

P = 128
D = 1024
T = 1024
NT = T // P
DC = D // P
HALF = 512
D_POOL = 512
N_HEADS = 8
DH = 64
WINDOWS = (2, 4, 8, 16)
NG = len(WINDOWS)
N_EXPERTS = 64
N_GROUPS = 8
PER_GROUP = N_EXPERTS // N_GROUPS
TOP_GROUPS = 4
TOP_K = 8
F = 256
FC = F // P
ROUTED_SCALE = 2.5
EPS = 1e-6
UNIT = 2048
UC = 256
TAB = P + 4
SKIP = 5000
LOWEST = -3.0e38
BIG = 1.0e30

C_C, C_ADA, C_GPM, C_GOM, C_GPF, C_GOF, C_PS, C_GMIX = 0, 8, 56, 64, 72, 80, 88, 92
N_PARAM = 100

BASE = 16512
KB = 1024
AT = 11


def build(nc, x, c, w_ada, b_ada, g_pre_mix, g_post_mix, g_pre_ffn, g_post_ffn, w_in, b_forget,
          w_pool, pool_scale, g_pool_out, g_attn_out, w_out, w_router, router_bias,
          w_gate, w_up, w_down, ws_gate, ws_up, ws_down, out, x1_dram, h2_dram, acc_dram):
    stack = ExitStack()

    def sem(name):
        return stack.enter_context(nc.semaphore(name))

    def at(name, kb, shape, dt):
        return nc.alloc_sbuf_tensor_at(name, shape, dt, offset=BASE + int(kb * KB))

    with stack:
        PS = stack.enter_context(nc.psum_tensor("PS", [P, 8, HALF], F32))

        ident = at("ident", 0, [P, P], F32)
        ones = at("ones", 0.5, [P, P], F32)
        pcol = at("pcol", 1, [P, P], F32)
        modc = at("modc", 1.5, [P, 48], F32)
        vecc = at("vecc", 1.75, [P, 6, DC], F32)
        epsc = at("epsc", 2, [P, 8], F32)
        ssum = at("ssum", 2.0625, [P, 64], F32)
        root = at("root", 2.3125, [P, 64], F32)
        rstd = at("rstd", 2.5625, [P, 64], F32)
        mmax = at("mmax", 2.8125, [P, 128], F32)
        negm = at("negm", 3.3125, [P, 64], F32)
        psum_row = at("prob_sum", 3.5625, [P, 64], F32)
        prec = at("prob_rec", 3.8125, [P, 64], F32)
        gidx = at("gather_rows", 4.0625, [P, TAB], I32)
        sidx = at("scatter_rows", 4.625, [P, TAB], I32)
        wtab = at("slot_weight", 5.1875, [P, TAB], F32)
        btab = at("block_table", 5.75, [P, 6, TAB], I32)
        etab = at("expert_table", 8.875, [P, TAB + 4], I32)
        bfc = at("b_forget_col", 9.4375, [P, 8], F32)
        gnow = at("gather_now", 9.5, [P, 2, 8], I32)
        snow = at("scatter_now", 9.5625, [P, 2, 8], I32)

        uqkv = at("uqkv", AT, [P, 16384], F32)
        hTh = at("hT_hi", AT + 64, [P, DC, T], F32R)
        hTl = at("hT_lo", AT + 96, [P, DC, T], F32R)
        wsh = at("w_hi", AT + 128, [P, 2, DC, P], F32R)
        wsl = at("w_lo", AT + 136, [P, 2, DC, P], F32R)
        vT = at("vT", AT + 144, [P, T], F32)
        NR = 4
        raw = at("raw", AT + 148, [P, NR, UNIT], F32)
        zf = at("zf", AT + 180, [P, T], F32)
        prow = at("prow", AT + 184, [P, P], F32)
        uT = uqkv[:, 0:4096].rearrange("p (g t) -> p g t", g=4)
        qT = uqkv[:, 4096:8192].rearrange("p (g t) -> p g t", g=4)
        kT = uqkv[:, 8192:12288].rearrange("p (g t) -> p g t", g=4)
        vr = uqkv[:, 12288:16384].rearrange("p (t f) -> p t f", t=NT)
        xin = uqkv[:, 8192:16384].rearrange("p (t d) -> p t d", t=NT)
        row_sm = uqkv[:, 0:D]
        row_bm = uqkv[:, D:2 * D]
        diag = [uqkv[:, 2048:3072].rearrange("p (c m) -> p c m", c=DC),
                uqkv[:, 3072:4096].rearrange("p (c m) -> p c m", c=DC)]
        wf = at("wf", AT + 188, [P, DC, P], F32)

        units = [("ada", u) for u in range(8)] + [("win", u) for u in range(8)] \
            + [("ada", u) for u in range(8, 24)]
        unit_at = {key: n for n, key in enumerate(units)}

        s_const = sem("s_const")
        s_prow = sem("s_prow")
        s_x = [sem(f"s_x_tile{t}") for t in range(NT)]
        s_raw = [sem(f"s_raw{i}") for i in range(NR)]
        s_wf0 = sem("s_wf0")
        s_wf = sem("s_wf")
        s_pt = sem("s_pt")
        s_pcol = sem("s_pcol")
        s_ada = sem("s_ada")
        s_ss = sem("s_ss")
        s_rt = sem("s_rt")
        s_rs = sem("s_rs")
        s_mod = sem("s_mod")
        s_diag = sem("s_diag")
        s_bc = sem("s_bc")
        s_row = sem("s_row")
        s_hx = sem("s_hx")
        s_h = sem("s_h")
        s_tr = sem("s_tr")
        s_hh = sem("s_hh")
        s_hl = sem("s_hl")
        s_wh = sem("s_wh")
        s_wl = sem("s_wl")
        s_pj = sem("s_pj")
        s_eva = sem("s_eva")
        s_evd = sem("s_evd")
        s_vt = sem("s_vt")
        s_va = sem("s_va")
        s_vd = sem("s_vd")
        s_bf = sem("s_bf")

        def raw_wait(eng, key):
            n = unit_at[key]
            eng.wait_ge(s_raw[n % NR], 16 * (n // NR + 1))
            return raw[:, n % NR, :]

        with nc.Block() as block:
            @block.sync
            def _(sp):
                rows = [(c.rearrange("b (r m) -> (b r) m", m=P), 8), (b_ada.rearrange("l (r m) -> (l r) m", m=P), 48)]
                rows += [(g.rearrange("l (r m) -> (l r) m", m=P), 8)
                         for g in (g_pre_mix, g_post_mix, g_pre_ffn, g_post_ffn)]
                rows += [(g.rearrange("l (r m) -> (l r) m", m=P), 4) for g in (pool_scale, g_pool_out, g_attn_out)]
                r0 = 0
                for src, n in rows:
                    sp.dma_start(prow[r0:r0 + n, :], src).then_inc(s_prow, 16)
                    r0 += n
                sp.dma_start(bfc[0:8, 0:1], b_forget.rearrange("l h -> h l")).then_inc(s_bf, 16)
                for n, (kind, u) in enumerate(units):
                    if n >= NR:
                        k, v = units[n - NR]
                        if k == "ada":
                            sp.wait_ge(s_ada, v + 1)
                        else:
                            sp.wait_ge(s_wh, 2 * v + 2)
                            sp.wait_ge(s_wl, 2 * v + 2)
                    w = w_ada if kind == "ada" else w_in
                    sp.dma_start(raw[:, n % NR, :].rearrange("p (c n) -> p c n", c=DC),
                                 w[0, :, u * UC:(u + 1) * UC].rearrange("(c p) n -> p c n", p=P)
                                 ).then_inc(s_raw[n % NR], 16)
                sp.wait_ge(s_bf, 16)

            @block.gpsimd
            def _(po):
                po.memset(ident[:], 0.0).then_inc(s_const, 1)
                po.memset(ones[:], 1.0).then_inc(s_const, 1)
                po.memset(epsc[:], EPS).then_inc(s_const, 1)
                po.wait_ge(s_const, 1)
                po.affine_select(out=ident[:], in_=ident[:], compare_op=ALU.not_equal, fill=1.0, base=0,
                                 pattern=[[-1, P]], channel_multiplier=1).then_inc(s_const, 1)
                po.memset(wf[:], 0.0).then_inc(s_wf0, 1)
                po.wait_ge(s_wf0, 1)
                po.dma_start(wf[:, :, 0:8], w_in[0, :, 2048:2056].rearrange("(c p) n -> p c n", p=P)).then_inc(s_wf, 16)
                po.wait_ge(s_row, 4)
                for t in range(NT):
                    po.wait_ge(s_hx, t + 1)
                    po.tensor_tensor(xin[:, t, :], xin[:, t, :], row_bm, ALU.add).then_inc(s_h, 1)
                po.wait_ge(s_wf, 16)

            @block.scalar
            def _(act):
                for t in range(NT):
                    act.dma_start(xin[:, t, :], x[0, t * P:(t + 1) * P, :]).then_inc(s_x[t], 16)
                act.wait_ge(s_const, 4)
                for t in range(NT):
                    act.wait_ge(s_x[t], 16)
                    if t:
                        act.wait_ge(s_ss, t)
                    act.activation(PS[:, 5:7, :].rearrange("p a b -> p (a b)"), xin[:, t, :], ACT.Square,
                                   accum_out=ssum[:, t:t + 1]).then_inc(s_ss, 1)
                act.wait_ge(s_ss, NT)
                act.activation(root[:, 0:NT], ssum[:, 0:NT], ACT.Sqrt, bias=epsc[:, 0:1], scale=1.0 / D).then_inc(s_rt, 1)
                act.wait_ge(s_bc, 2)
                act.copy(row_bm, PS[:, 2:4, :].rearrange("p a b -> p (a b)")).then_inc(s_row, 2)

                def split(f):
                    if f < 16:
                        src = raw_wait(act, ("win", f // 2)).rearrange("p (c n) -> p c n", c=DC)[:, :, (f % 2) * P:(f % 2 + 1) * P]
                    else:
                        src = wf[:]
                        act.wait_ge(s_wf, 16)
                    if f >= 2:
                        act.wait_ge(s_pj, 2 * (f - 1))
                    act.copy(wsh[:, f % 2], src).then_inc(s_wh, 1)

                for t in range(NT):
                    for h in range(2):
                        act.wait_ge(s_tr, 2 * t + h + 1)
                        act.copy(hTh[:, 4 * h:4 * h + 4, t * P:(t + 1) * P],
                                 PS[:, (t % 2) * 2 + h, :].rearrange("p (c m) -> p c m", c=4)).then_inc(s_hh, 1)
                    if t < 2:
                        split(t)
                for f in range(17):
                    if f + 1 < 17 and f >= 1:
                        split(f + 1)
                    act.wait_ge(s_pj, 2 * f + 1)
                    src = PS[:, (f % 2) * 2, :]
                    if f < 12:
                        if 4 <= f < 8:
                            act.mul(uqkv[:, f * T:f * T + HALF], src, DH ** -0.5).then_inc(s_eva, 1)
                        else:
                            act.copy(uqkv[:, f * T:f * T + HALF], src).then_inc(s_eva, 1)
                    elif f < 16:
                        if f > 12:
                            act.wait_ge(s_vt, f - 12)
                        act.copy(vT[:, 0:HALF], src).then_inc(s_eva, 1)
                    else:
                        act.copy(zf[0:8, 0:HALF], src[0:8, :]).then_inc(s_eva, 1)
                    if 12 < f <= 16:
                        fc = f - 13
                        act.wait_ge(s_vt, fc + 1)
                        act.copy(vr[:, 0:4, fc * P:(fc + 1) * P], PS[:, 4, :].rearrange("p (t m) -> p t m", t=4)).then_inc(s_va, 1)

            @block.vector
            def _(v):
                v.wait_ge(s_pt, 1)
                v.tensor_copy(pcol[:, 0:N_PARAM], PS[:, 7, 0:N_PARAM]).then_inc(s_pcol, 1)
                v.wait_ge(s_rt, 1)
                v.reciprocal(rstd[:, 0:NT], root[:, 0:NT]).then_inc(s_rs, 1)
                v.wait_ge(s_ada, 8)
                v.wait_ge(s_pcol, 1)
                v.tensor_tensor(modc[:, 0:16], PS[:, 7, P:P + 16], pcol[:, C_ADA:C_ADA + 16], ALU.add).then_inc(s_mod, 1)
                v.wait_ge(s_mod, 1)
                v.scalar_tensor_tensor(vecc[:, 0, :], modc[:, 8:16], 1.0, pcol[:, C_GPM:C_GPM + 8],
                                       ALU.add, ALU.mult).then_inc(s_mod, 1)
                v.wait_ge(s_mod, 2)
                v.wait_ge(s_const, 4)
                for i, col in enumerate((vecc[:, 0, :], modc[:, 0:8])):
                    v.tensor_tensor(diag[i], ident[:, None, :].broadcast_to([P, DC, P]),
                                    col[:, :, None].broadcast_to([P, DC, P]), ALU.mult).then_inc(s_diag, 1)
                v.wait_ge(s_bc, 1)
                v.tensor_copy(row_sm, PS[:, 0:2, :].rearrange("p a b -> p (a b)")).then_inc(s_row, 2)
                v.wait_ge(s_row, 4)
                v.wait_ge(s_rs, 1)
                for t in range(NT):
                    v.scalar_tensor_tensor(xin[:, t, :], xin[:, t, :], rstd[:, t:t + 1], row_sm,
                                           ALU.mult, ALU.mult).then_inc(s_hx, 1)

                def split(f):
                    if f < 16:
                        src = raw_wait(v, ("win", f // 2)).rearrange("p (c n) -> p c n", c=DC)[:, :, (f % 2) * P:(f % 2 + 1) * P]
                    else:
                        src = wf[:]
                        v.wait_ge(s_wf, 16)
                    v.wait_ge(s_wh, f + 1)
                    if f >= 2:
                        v.wait_ge(s_pj, 2 * (f - 1))
                    v.tensor_tensor(wsl[:, f % 2], src, wsh[:, f % 2].bitcast(F32), ALU.subtract).then_inc(s_wl, 1)

                for t in range(NT):
                    for h in range(2):
                        v.wait_ge(s_hh, 2 * t + h + 1)
                        dst = (slice(None), slice(4 * h, 4 * h + 4), slice(t * P, (t + 1) * P))
                        v.tensor_tensor(hTl[dst], PS[:, (t % 2) * 2 + h, :].rearrange("p (c m) -> p c m", c=4),
                                        hTh[dst].bitcast(F32), ALU.subtract).then_inc(s_hl, 1)
                    if t < 2:
                        split(t)
                for f in range(17):
                    if f + 1 < 17 and f >= 1:
                        split(f + 1)
                    v.wait_ge(s_pj, 2 * f + 2)
                    src = PS[:, (f % 2) * 2 + 1, :]
                    if f < 12:
                        if 4 <= f < 8:
                            v.tensor_scalar(uqkv[:, f * T + HALF:(f + 1) * T], src, DH ** -0.5, None, ALU.mult).then_inc(s_evd, 1)
                        else:
                            v.tensor_copy(uqkv[:, f * T + HALF:(f + 1) * T], src).then_inc(s_evd, 1)
                    elif f < 16:
                        if f > 12:
                            v.wait_ge(s_vt, f - 12)
                        v.tensor_copy(vT[:, HALF:T], src).then_inc(s_evd, 1)
                    else:
                        v.tensor_copy(zf[0:8, HALF:T], src[0:8, :]).then_inc(s_evd, 1)
                    if 12 < f <= 16:
                        fc = f - 13
                        v.wait_ge(s_vt, fc + 1)
                        v.tensor_copy(vr[:, 4:8, fc * P:(fc + 1) * P], PS[:, 5, :].rearrange("p (t m) -> p t m", t=4)).then_inc(s_vd, 1)
                v.wait_ge(s_ada, 24)
                v.tensor_tensor(modc[:, 16:48], PS[:, 7, P + 16:P + 48], pcol[:, C_ADA + 16:C_ADA + 48], ALU.add).then_inc(s_mod, 1)
                v.wait_ge(s_mod, 3)
                v.tensor_tensor(vecc[:, 1, :], modc[:, 16:24], pcol[:, C_GOM:C_GOM + 8], ALU.mult).then_inc(s_mod, 1)
                v.scalar_tensor_tensor(vecc[:, 2, :], modc[:, 32:40], 1.0, pcol[:, C_GPF:C_GPF + 8],
                                       ALU.add, ALU.mult).then_inc(s_mod, 1)
                v.tensor_tensor(vecc[:, 3, :], modc[:, 40:48], pcol[:, C_GOF:C_GOF + 8], ALU.mult).then_inc(s_mod, 1)
                v.wait_ge(s_mod, 6)

            @block.tensor
            def _(pe):
                def gemv(u):
                    w = raw_wait(pe, ("ada", u)).rearrange("p (c n) -> p c n", c=DC)
                    for fc in range(2):
                        for dc in range(DC):
                            mm = pe.matmul(PS[:, 7, P + 2 * u + fc:P + 2 * u + fc + 1], w[:, dc, fc * P:(fc + 1) * P],
                                           pcol[:, C_C + dc:C_C + dc + 1], start=(dc == 0), stop=(dc == DC - 1))
                    mm.then_inc(s_ada, 1)

                pe.wait_ge(s_const, 4)
                pe.wait_ge(s_prow, 144)
                pe.transpose(PS[:, 7, 0:N_PARAM], prow[0:N_PARAM, :], ident[0:N_PARAM, 0:N_PARAM]).then_inc(s_pt, 1)
                pe.wait_ge(s_pcol, 1)
                for u in range(8):
                    gemv(u)
                for i in range(2):
                    pe.wait_ge(s_diag, i + 1)
                    for h in range(2):
                        mm = pe.matmul(PS[:, 2 * i + h, :], ones[:], diag[i][:, 4 * h:4 * h + 4, :], start=True, stop=True)
                    mm.then_inc(s_bc, 1)
                for t in range(NT):
                    pe.wait_ge(s_h, t + 1)
                    for h in range(2):
                        if t >= 2:
                            pe.wait_ge(s_hl, 2 * (t - 2) + h + 1)
                        for q in range(4):
                            dc = 4 * h + q
                            mm = pe.transpose(PS[:, (t % 2) * 2 + h, q * P:(q + 1) * P], xin[:, t, dc * P:(dc + 1) * P], ident[:])
                        mm.then_inc(s_tr, 1)
                pe.wait_ge(s_hl, 2 * NT)

                def v_transposes(fc):
                    pe.wait_ge(s_eva, 13 + fc)
                    pe.wait_ge(s_evd, 13 + fc)
                    if fc:
                        pe.wait_ge(s_va, fc)
                        pe.wait_ge(s_vd, fc)
                    for t in range(NT):
                        mm = pe.transpose(PS[:, 4 + t // 4, (t % 4) * P:(t % 4 + 1) * P], vT[:, t * P:(t + 1) * P], ident[:])
                    mm.then_inc(s_vt, 1)

                for f in range(17):
                    pe.wait_ge(s_wh, f + 1)
                    pe.wait_ge(s_wl, f + 1)
                    if f >= 2:
                        pe.wait_ge(s_eva, f - 1)
                        pe.wait_ge(s_evd, f - 1)
                    if 12 < f <= 16:
                        v_transposes(f - 13)
                    for h in range(2):
                        n = 0
                        for dc in range(DC):
                            for wt, ht in ((wsh, hTh), (wsh, hTl), (wsl, hTh)):
                                mm = pe.matmul(PS[:, (f % 2) * 2 + h, :], wt[:, f % 2, dc, :], ht[:, dc, h * HALF:(h + 1) * HALF],
                                               start=(n == 0), stop=(n == 3 * DC - 1))
                                n += 1
                        mm.then_inc(s_pj, 1)
                for u in range(8, 24):
                    gemv(u)

        ymix = at("ymix", AT + 64, [P, NT, D], F32)
        woraw = at("woraw", AT + 96, [P, DC, D], F32)
        psrow = at("psrow", AT + 128, [P, D_POOL], F32)
        nckb = at("nckb", AT + 130, [P, 2, T], F32)
        nckd = at("nckd", AT + 138, [P, 2, T], F32)
        Sb = at("Sb", AT + 146, [P, 2, T], F32)
        Pm = at("Pm", AT + 154, [P, 2, T], F32)
        PT = at("PT", AT + 162, [P, 2, NT, P], F32)
        pw = [at("pwA", AT + 170, [P, T], F32), at("pwB", AT + 174, [P, T], F32)]
        wpl = at("wpl", AT + 178, [P, NG, P], F32)
        cum = zf
        sel8 = at("sel8", AT + 184, [P, N_HEADS, P], F32)
        lz = at("lz", AT + 188, [P, 2, T], F32)
        diag4 = at("diag4", AT + 188, [P, 4, P], F32)
        counti = at("counti", 9.75, [P, 16], I32)
        countf = at("countf", 9.8125, [P, 16], F32)
        rinv = at("rinv", 9.875, [P, 16], F32)

        s_c2 = sem("s_c2")
        s_wo = sem("s_wo")
        s_wp = sem("s_wp")
        s_lf = sem("s_lf")
        s_la = sem("s_la")
        s_cum = sem("s_cum")
        s_nk = sem("s_nk")
        s_nb = sem("s_nb")
        s_nd = sem("s_nd")
        s_s = sem("s_s")
        s_t1 = sem("s_t1")
        s_t2 = sem("s_t2")
        s_ng = sem("s_ng")
        s_ex = sem("s_ex")
        s_pT = sem("s_pT")
        s_pta = sem("s_pta")
        s_ptd = sem("s_ptd")
        s_pv = sem("s_pv")
        s_rc = sem("s_rc")
        s_rr = sem("s_rr")
        s_oe = sem("s_oe")
        s_pw = sem("s_pw")
        s_po = sem("s_po")
        s_yp = sem("s_yp")
        s_ye = sem("s_ye")
        s_dg2 = sem("s_dg2")
        s_b2 = sem("s_b2")
        s_r2 = sem("s_r2")
        s_sm = sem("s_sm")
        s_md = sem("s_md")

        steps = [(h, q) for h in range(N_HEADS) for q in range(NT)]
        NS = len(steps)

        def taken(i, act):
            return (i + 1) // 2 if act else (i + 2) // 2

        with nc.Block() as block:
            @block.sync
            def _(sp):
                sp.dma_start(wpl[:], w_pool[0].rearrange("g c d -> c g d")).then_inc(s_wp, 16)
                for q in range(4):
                    sp.dma_start(woraw[:, 2 * q:2 * q + 2, :],
                                 w_out[0, 2 * q * P:(2 * q + 2) * P, :].rearrange("(c p) n -> p c n", p=P)).then_inc(s_wo, 16)
                sp.wait_ge(s_wp, 16)
                sp.wait_ge(s_wo, 64)

            @block.gpsimd
            def _(po):
                po.memset(sel8[0:8], 0.0).then_inc(s_c2, 1)
                po.wait_ge(s_c2, 1)
                po.affine_select(out=sel8[0:8], in_=sel8[0:8], compare_op=ALU.not_equal, fill=-1.0, base=0,
                                 pattern=[[-1, N_HEADS], [0, P]], channel_multiplier=1).then_inc(s_c2, 1)
                po.iota(counti[:], [[1, 16]], base=1, channel_multiplier=0).then_inc(s_c2, 1)
                done = [0]

                def link(ins):
                    done[0] += 1
                    ins.then_inc(s_pw, 1)
                    po.wait_ge(s_pw, done[0])

                def diagonal(h):
                    if h >= 2:
                        po.wait_ge(s_t1, 8 * (h - 1))
                    po.wait_ge(s_nb, 2 * h + 2)
                    po.affine_select(out=nckd[:, h % 2, :].rearrange("p (q m) -> p q m", q=NT),
                                     in_=nckb[:, h % 2, :].rearrange("p (q m) -> p q m", q=NT),
                                     compare_op=ALU.is_ge, fill=-BIG, base=0,
                                     pattern=[[0, NT], [-1, P]], channel_multiplier=1).then_inc(s_nd, 1)

                po.wait_ge(s_rr, 1)
                for g, w in enumerate(WINDOWS):
                    diagonal(g)
                    cur = uT[:, g, :]
                    s, k = 1, 0
                    while s < w:
                        nxt = pw[k % 2]
                        link(po.tensor_copy(nxt[:, 0:s], cur[:, 0:s]))
                        link(po.tensor_tensor(nxt[:, s:T], cur[:, s:T], cur[:, 0:T - s], ALU.add))
                        cur = nxt
                        s, k = 2 * s, k + 1
                    nxt = pw[k % 2]
                    link(po.tensor_scalar(nxt[:, w:T], cur[:, w:T], 1.0 / w, None, ALU.mult))
                    link(po.tensor_tensor(nxt[:, 0:w], cur[:, 0:w], rinv[:, 0:w], ALU.mult))
                    link(po.tensor_tensor(uT[:, g, :], nxt[:], uT[:, g, :], ALU.subtract))
                po.sem_inc(s_po, 1)
                for h in range(NG, N_HEADS):
                    diagonal(h)

            @block.scalar
            def _(act):
                act.wait_ge(s_lf, 3)
                act.activation(lz[0:8, 0, :], lz[0:8, 0, :], ACT.Exp, scale=-1.0).then_inc(s_la, 1)
                act.wait_ge(s_la, 1)
                act.activation(lz[0:8, 0, :], lz[0:8, 0, :], ACT.Ln, bias=1.0).then_inc(s_la, 1)

                def key_term(n):
                    h, half = divmod(n, 2)
                    if h >= 2:
                        act.wait_ge(s_t2, 8 * (h - 1))
                        act.wait_ge(s_nd, h - 1)
                    act.wait_ge(s_nk, n + 1)
                    act.copy(nckb[:, h % 2, half * HALF:(half + 1) * HALF], PS[:, 6, :]).then_inc(s_nb, 1)

                def transposed(i):
                    act.wait_ge(s_pT, i + 1)
                    q = steps[i][1]
                    if i >= 2:
                        act.wait_ge(s_pv, i - 1)
                    act.copy(PT[:, i % 2, 0:q + 1, :], PS[:, 4:6, :].rearrange("p a (b m) -> p (a b) m", m=P)[:, 0:q + 1, :]).then_inc(s_pta, 1)

                key_term(0)
                key_term(1)
                for i, (h, q) in enumerate(steps):
                    act.wait_ge(s_ng, i + 1)
                    if i >= 2:
                        act.wait_ge(s_pT, i - 1)
                    w = (q + 1) * P
                    act.activation(Pm[:, i % 2, 0:w], Sb[:, i % 2, 0:w], ACT.Exp, bias=negm[:, i:i + 1],
                                   accum_out=psum_row[:, i:i + 1]).then_inc(s_ex, 1)
                    if i >= 1 and (i - 1) % 2 == 1:
                        transposed(i - 1)
                    if h + 1 < N_HEADS and q in (4, 6):
                        key_term(2 * (h + 1) + (q - 4) // 2)
                transposed(NS - 1)
                for t in range(NT):
                    act.wait_ge(s_oe, 8 * 7 + t + 1)
                    if t:
                        act.wait_ge(s_sm, 2 * t)
                    act.activation(Pm[:, 0, 0:HALF], ymix[:, t, HALF:D], ACT.Square, accum_out=ssum[:, 8 + t:9 + t]).then_inc(s_sm, 1)
                    act.wait_ge(s_ye, t + 1)
                    act.activation(Pm[:, 1, 0:HALF], ymix[:, t, 0:HALF], ACT.Square, accum_out=ssum[:, t:t + 1]).then_inc(s_sm, 1)

            @block.vector
            def _(v):
                v.wait_ge(s_c2, 3)
                v.tensor_copy(countf[:], counti[:]).then_inc(s_md, 1)
                v.wait_ge(s_md, 1)
                v.reciprocal(rinv[:], countf[:]).then_inc(s_rr, 1)
                v.tensor_scalar(zf[0:8, :], zf[0:8, :], bfc[0:8, 0:1], None, ALU.add).then_inc(s_lf, 1)
                v.wait_ge(s_lf, 1)
                v.scalar_tensor_tensor(lz[0:8, 0, :], zf[0:8, :], -1.0, zf[0:8, :], ALU.mult, ALU.max).then_inc(s_lf, 1)
                v.tensor_scalar(lz[0:8, 1, :], zf[0:8, :], 0.0, None, ALU.min).then_inc(s_lf, 1)
                v.wait_ge(s_la, 2)
                v.wait_ge(s_lf, 3)
                v.tensor_tensor(lz[0:8, 1, :], lz[0:8, 1, :], lz[0:8, 0, :], ALU.subtract).then_inc(s_lf, 1)
                v.wait_ge(s_lf, 4)
                v.memset(lz[0:8, 0, :], 1.0).then_inc(s_lf, 1)
                v.wait_ge(s_lf, 5)
                v.tensor_tensor_scan(cum[0:8, :], lz[0:8, 0, :], lz[0:8, 1, :], 0.0, ALU.mult, ALU.add).then_inc(s_cum, 1)
                v.wait_ge(s_cum, 1)
                v.tensor_tensor(diag4[:], ident[:, None, :].broadcast_to([P, 4, P]),
                                pcol[:, C_PS:C_PS + 4][:, :, None].broadcast_to([P, 4, P]), ALU.mult).then_inc(s_dg2, 1)
                v.wait_ge(s_b2, 1)
                v.tensor_copy(psrow[:], PS[:, 5, :]).then_inc(s_r2, 1)

                def score(i):
                    h, q = steps[i]
                    v.wait_ge(s_s, i + 1)
                    v.wait_ge(s_nd, h + 1)
                    if i >= 2:
                        v.wait_ge(s_ex, i - 1)
                    flat = PS[:, (i % 2) * 2:(i % 2) * 2 + 2, :].rearrange("p a b -> p (a b)")
                    w = q * P
                    first = v.tensor_tensor_reduce(Sb[:, i % 2, w:w + P], flat[:, w:w + P], nckd[:, h % 2, w:w + P], 1.0, LOWEST,
                                                   ALU.add, ALU.max, mmax[:, 2 * (i % 32):2 * (i % 32) + 1])
                    first.then_inc(s_t1, 1)
                    v.wait_ge(s_t1, i + 1)
                    col = 2 * (i % 32)
                    if q:
                        v.tensor_tensor_reduce(Sb[:, i % 2, 0:w], flat[:, 0:w], nckb[:, h % 2, 0:w], 1.0, mmax[:, col:col + 1],
                                               ALU.add, ALU.max, mmax[:, col + 1:col + 2]).then_inc(s_t2, 1)
                        col += 1
                    else:
                        v.engine_nop().then_inc(s_t2, 1)
                    v.wait_ge(s_t2, i + 1)
                    v.tensor_scalar(negm[:, i:i + 1], mmax[:, col:col + 1], -1.0, None, ALU.mult).then_inc(s_ng, 1)

                def transposed(i):
                    v.wait_ge(s_pT, i + 1)
                    q = steps[i][1]
                    if i >= 2:
                        v.wait_ge(s_pv, i - 1)
                    v.tensor_copy(PT[:, i % 2, 0:q + 1, :], PS[:, 4:6, :].rearrange("p a (b m) -> p (a b) m", m=P)[:, 0:q + 1, :]).then_inc(s_ptd, 1)

                def output(i):
                    h, q = steps[i]
                    v.wait_ge(s_ex, i + 1)
                    v.reciprocal(prec[:, i:i + 1], psum_row[:, i:i + 1]).then_inc(s_rc, 1)
                    v.wait_ge(s_rc, i + 1)
                    v.wait_ge(s_pv, i + 1)
                    v.tensor_scalar(ymix[:, q, HALF + h * DH:HALF + (h + 1) * DH], PS[:, 7 - i % 2, 0:DH],
                                    prec[:, i:i + 1], None, ALU.mult).then_inc(s_oe, 1)

                score(0)
                for i in range(NS):
                    if i + 1 < NS:
                        score(i + 1)
                    if i % 2 == 0:
                        transposed(i)
                    if i >= 2:
                        output(i - 2)
                output(NS - 2)
                output(NS - 1)
                for t in range(NT):
                    v.wait_ge(s_yp, t + 1)
                    v.tensor_tensor(ymix[:, t, 0:HALF], PS[:, t % 2, :], psrow[:], ALU.mult).then_inc(s_ye, 1)

            @block.tensor
            def _(pe):
                pe.wait_ge(s_dg2, 1)
                pe.matmul(PS[:, 5, :], ones[:], diag4[:], start=True, stop=True).then_inc(s_b2, 1)
                pe.wait_ge(s_r2, 1)

                key_terms = [0]

                def key_term(n):
                    h, half = divmod(n, 2)
                    if n:
                        pe.wait_ge(s_nb, n)
                    key_terms[0] = n + 1
                    pe.matmul(PS[:, 6, :], sel8[0:8, h, :], cum[0:8, half * HALF:(half + 1) * HALF], start=True, stop=True).then_inc(s_nk, 1)

                def score(i):
                    h, q = steps[i]
                    if i >= 2:
                        pe.wait_ge(s_t1, i - 1)
                        pe.wait_ge(s_t2, i - 1)
                    pb = (h % 2) * DH
                    w = (q + 1) * P
                    for k0 in range(0, w, HALF):
                        n = min(HALF, w - k0)
                        mm = pe.matmul(PS[:, (i % 2) * 2 + k0 // HALF, 0:n], qT[pb:pb + DH, h // 2, q * P:(q + 1) * P],
                                       kT[pb:pb + DH, h // 2, k0:k0 + n], start=True, stop=True)
                    mm.then_inc(s_s, 1)

                def transposes(i):
                    q = steps[i][1]
                    pe.wait_ge(s_ex, i + 1)
                    if i >= 1:
                        pe.wait_ge(s_pta, taken(i - 1, True))
                        pe.wait_ge(s_ptd, taken(i - 1, False))
                    for k in range(q + 1):
                        mm = pe.transpose(PS[:, 4 + k // 4, (k % 4) * P:(k % 4 + 1) * P], Pm[:, i % 2, k * P:(k + 1) * P], ident[:])
                    mm.then_inc(s_pT, 1)

                def values(i):
                    h, q = steps[i]
                    pe.wait_ge(s_pta, taken(i, True))
                    pe.wait_ge(s_ptd, taken(i, False))
                    if i >= 2:
                        pe.wait_ge(s_oe, i - 1)
                    if i % 2:
                        pe.wait_ge(s_nb, key_terms[0])
                    for k in range(q + 1):
                        mm = pe.matmul(PS[:, 7 - i % 2, 0:DH], PT[:, i % 2, k, :], vr[:, k, h * DH:(h + 1) * DH],
                                       start=(k == 0), stop=(k == q))
                    mm.then_inc(s_pv, 1)

                pe.wait_ge(s_c2, 2)
                pe.wait_ge(s_cum, 1)
                key_term(0)
                key_term(1)
                score(0)
                score(1)
                for i, (h, q) in enumerate(steps):
                    transposes(i)
                    if i + 2 < NS:
                        score(i + 2)
                    if h + 1 < N_HEADS and q in (3, 5):
                        pe.wait_ge(s_oe, i - 1)
                        key_term(2 * (h + 1) + (q - 3) // 2)
                    if i:
                        values(i - 1)
                values(NS - 1)
                pe.wait_ge(s_wp, 16)
                pe.wait_ge(s_po, 1)
                pe.wait_ge(s_t2, NS)
                for t in range(NT):
                    if t >= 2:
                        pe.wait_ge(s_ye, t - 1)
                    for g in range(NG):
                        mm = pe.matmul(PS[:, t % 2, g * P:(g + 1) * P], uT[:, g, t * P:(t + 1) * P], wpl[:, g, :], start=True, stop=True)
                    mm.then_inc(s_yp, 1)

        woh = at("wo_hi", AT, [P, DC, D], F32R)
        wol = at("wo_lo", AT + 32, [P, DC, D], F32R)
        xt = at("xt", AT + 96, [P, 2, D], F32)
        x1 = at("x1", AT + 104, [P, 2, D], F32)
        h2 = at("h2", AT + 112, [P, 2, D], F32)
        mx = at("mx", AT + 120, [P, 2, D], F32)
        rows3 = at("rows3", AT + 128, [P, 4, D], F32)
        diag3 = at("diag3", AT + 144, [P, 2, DC, P], F32)
        mTh = at("mT_hi", AT + 152, [P, 2, DC, P], F32R)
        mTl = at("mT_lo", AT + 160, [P, 2, DC, P], F32R)
        gTh = at("gT_hi", AT + 168, [P, 2, DC, P], F32R)
        gTl = at("gT_lo", AT + 176, [P, 2, DC, P], F32R)
        wrr = at("wr_raw", AT + 184, [P, DC, N_EXPERTS], F32)
        wrh = at("wr_hi", AT + 186, [P, DC, N_EXPERTS], F32R)
        wrl = at("wr_lo", AT + 188, [P, DC, N_EXPERTS], F32R)
        score_t = at("score_t", AT + 190, [P, NT, N_EXPERTS], F32)
        junk = at("junk", AT + 192, [P, D], F32)
        GM, SF, BF, GX = range(4)

        s_wr = sem("s_wr")
        s_dg3 = sem("s_dg3")
        s_b3 = sem("s_b3")
        s_r3 = sem("s_r3")
        s_q3 = sem("s_q3")
        s_m3 = sem("s_m3")
        s_woh = sem("s_woh")
        s_wol = sem("s_wol")
        s_wrh = sem("s_wrh")
        s_wrl = sem("s_wrl")
        s_mx = sem("s_mx")
        s_tm = sem("s_tm")
        s_tmh = sem("s_tmh")
        s_tml = sem("s_tml")
        s_wp3 = sem("s_wp3")
        s_sq1 = sem("s_sq1")
        s_rt1 = sem("s_rt1")
        s_rs1 = sem("s_rs1")
        s_xa = sem("s_xa")
        s_x1 = sem("s_x1")
        s_sq2 = sem("s_sq2")
        s_rt2 = sem("s_rt2")
        s_rs2 = sem("s_rs2")
        s_ha = sem("s_ha")
        s_h2 = sem("s_h2")
        s_th = sem("s_th")
        s_thh = sem("s_thh")
        s_thl = sem("s_thl")
        s_lg = sem("s_lg")
        s_xl = [sem("s_xl0"), sem("s_xl1")]
        s_sx = [sem("s_sx0"), sem("s_sx1")]
        s_sh = [sem("s_sh0"), sem("s_sh1")]
        s_sig = sem("s_sig")

        def flat2(b):
            return PS[:, b:b + 2, :].rearrange("p a b -> p (a b)")

        def quads(b):
            return PS[:, b, :].rearrange("p (c m) -> p c m", c=4)

        with nc.Block() as block:
            @block.sync
            def _(sp):
                sp.dma_start(wrr[:], w_router[0].rearrange("(c p) n -> p c n", p=P)).then_inc(s_wr, 16)
                sp.wait_ge(s_woh, DC)
                sp.wait_ge(s_wol, DC)
                for t in range(2):
                    sp.dma_start(xt[:, t, :], x[0, t * P:(t + 1) * P, :]).then_inc(s_xl[t], 16)
                for t in range(NT):
                    b = t % 2
                    sp.wait_ge(s_x1, t + 1)
                    sp.dma_start(x1_dram[t * P:(t + 1) * P, :], x1[:, b, :]).then_inc(s_sx[b], 16)
                    if t + 2 < NT:
                        sp.dma_start(xt[:, b, :], x[0, (t + 2) * P:(t + 3) * P, :]).then_inc(s_xl[b], 16)
                    sp.wait_ge(s_h2, t + 1)
                    sp.dma_start(h2_dram[t * P:(t + 1) * P, :], h2[:, b, :]).then_inc(s_sh[b], 16)
                for b in range(2):
                    sp.wait_ge(s_sx[b], 16 * NT // 2)
                    sp.wait_ge(s_sh[b], 16 * NT // 2)

            @block.gpsimd
            def _(po):
                for t in range(NT):
                    b = t % 2
                    po.wait_ge(s_xa, t + 1)
                    po.wait_ge(s_xl[b], 16 * (t // 2 + 1))
                    po.tensor_tensor(x1[:, b, :], x1[:, b, :], xt[:, b, :], ALU.add).then_inc(s_x1, 1)
                    po.wait_ge(s_ha, t + 1)
                    po.tensor_tensor(h2[:, b, :], h2[:, b, :], rows3[:, BF, :], ALU.add).then_inc(s_h2, 1)

            @block.scalar
            def _(act):
                act.activation(root[:, 8:24], ssum[:, 0:16], ACT.Sqrt, bias=epsc[:, 0:1], scale=1.0 / HALF).then_inc(s_q3, 1)
                for dc in range(DC):
                    act.copy(woh[:, dc, :], woraw[:, dc, :]).then_inc(s_woh, 1)
                act.wait_ge(s_wr, 16)
                act.copy(wrh[:], wrr[:]).then_inc(s_wrh, 1)

                def mixed(t):
                    b = t % 2
                    for h in range(2):
                        act.wait_ge(s_tm, 2 * t + h + 1)
                        if t >= 2:
                            act.wait_ge(s_wp3, t - 1)
                        act.copy(mTh[:, b, 4 * h:4 * h + 4, :], quads(h)).then_inc(s_tmh, 1)

                def normed(t):
                    b = t % 2
                    for h in range(2):
                        act.wait_ge(s_th, 2 * t + h + 1)
                        if t >= 2:
                            act.wait_ge(s_lg, t - 1)
                        act.copy(gTh[:, b, 4 * h:4 * h + 4, :], quads(4 + h)).then_inc(s_thh, 1)

                mixed(0)
                for t in range(NT):
                    b = t % 2
                    if t + 1 < NT:
                        mixed(t + 1)
                    if t:
                        normed(t - 1)
                    act.wait_ge(s_wp3, t + 1)
                    act.activation(junk[:], flat2(2), ACT.Square, accum_out=ssum[:, 16 + t:17 + t]).then_inc(s_sq1, 1)
                    act.wait_ge(s_sq1, 2 * t + 1)
                    act.activation(root[:, 24 + t:25 + t], ssum[:, 16 + t:17 + t], ACT.Sqrt, bias=epsc[:, 0:1], scale=1.0 / D).then_inc(s_rt1, 1)
                    act.wait_ge(s_x1, t + 1)
                    act.activation(junk[:], x1[:, b, :], ACT.Square, accum_out=ssum[:, 24 + t:25 + t]).then_inc(s_sq1, 1)
                    act.wait_ge(s_sq1, 2 * t + 2)
                    act.activation(root[:, 32 + t:33 + t], ssum[:, 24 + t:25 + t], ACT.Sqrt, bias=epsc[:, 0:1], scale=1.0 / D).then_inc(s_rt2, 1)
                normed(NT - 1)
                act.wait_ge(s_lg, NT)
                act.activation(score_t[:], PS[:, 6, :].rearrange("p (t e) -> p t e", t=NT), ACT.Sigmoid).then_inc(s_sig, 1)

            @block.vector
            def _(v):
                v.wait_ge(s_q3, 1)
                v.reciprocal(rstd[:, 8:24], root[:, 8:24]).then_inc(s_m3, 1)
                cols = (vecc[:, 1, :], vecc[:, 2, :], modc[:, 24:32], pcol[:, C_GMIX:C_GMIX + 8])
                for i, col in enumerate(cols):
                    if i >= 2:
                        v.wait_ge(s_b3, i - 1)
                    v.tensor_tensor(diag3[:, i % 2], ident[:, None, :].broadcast_to([P, DC, P]),
                                    col[:, :, None].broadcast_to([P, DC, P]), ALU.mult).then_inc(s_dg3, 1)
                    if i:
                        v.wait_ge(s_b3, i)
                        v.tensor_copy(rows3[:, i - 1, :], flat2(((i - 1) % 2) * 2)).then_inc(s_r3, 1)
                v.wait_ge(s_b3, 4)
                v.tensor_copy(rows3[:, 3, :], flat2(2)).then_inc(s_r3, 1)
                v.wait_ge(s_r3, 4)
                for dc in range(DC):
                    v.wait_ge(s_woh, dc + 1)
                    v.tensor_tensor(wol[:, dc, :], woraw[:, dc, :], woh[:, dc, :].bitcast(F32), ALU.subtract).then_inc(s_wol, 1)
                v.wait_ge(s_wrh, 1)
                v.tensor_tensor(wrl[:], wrr[:], wrh[:].bitcast(F32), ALU.subtract).then_inc(s_wrl, 1)
                v.wait_ge(s_m3, 1)
                v.wait_ge(s_wol, DC)

                def scale_mixed(t):
                    b = t % 2
                    if t >= 2:
                        v.wait_ge(s_tm, 2 * (t - 1))
                    v.scalar_tensor_tensor(mx[:, b, 0:HALF], ymix[:, t, 0:HALF], rstd[:, 8 + t:9 + t], rows3[:, GX, 0:HALF],
                                           ALU.mult, ALU.mult).then_inc(s_mx, 1)
                    v.scalar_tensor_tensor(mx[:, b, HALF:D], ymix[:, t, HALF:D], rstd[:, 16 + t:17 + t], rows3[:, GX, HALF:D],
                                           ALU.mult, ALU.mult).then_inc(s_mx, 1)

                def mixed(t):
                    b = t % 2
                    for h in range(2):
                        v.wait_ge(s_tmh, 2 * t + h + 1)
                        v.tensor_tensor(mTl[:, b, 4 * h:4 * h + 4, :], quads(h), mTh[:, b, 4 * h:4 * h + 4, :].bitcast(F32),
                                        ALU.subtract).then_inc(s_tml, 1)

                def normed(t):
                    b = t % 2
                    for h in range(2):
                        v.wait_ge(s_thh, 2 * t + h + 1)
                        v.tensor_tensor(gTl[:, b, 4 * h:4 * h + 4, :], quads(4 + h), gTh[:, b, 4 * h:4 * h + 4, :].bitcast(F32),
                                        ALU.subtract).then_inc(s_thl, 1)

                scale_mixed(0)
                scale_mixed(1)
                mixed(0)
                for t in range(NT):
                    b = t % 2
                    if t + 1 < NT:
                        mixed(t + 1)
                    if t + 2 < NT:
                        scale_mixed(t + 2)
                    if t:
                        normed(t - 1)
                    v.wait_ge(s_rt1, t + 1)
                    v.reciprocal(rstd[:, 24 + t:25 + t], root[:, 24 + t:25 + t]).then_inc(s_rs1, 1)
                    v.wait_ge(s_rs1, t + 1)
                    if t >= 2:
                        v.wait_ge(s_sx[b], 16 * (t // 2))
                    v.scalar_tensor_tensor(x1[:, b, :], flat2(2), rstd[:, 24 + t:25 + t], rows3[:, GM, :],
                                           ALU.mult, ALU.mult).then_inc(s_xa, 1)
                    v.wait_ge(s_rt2, t + 1)
                    v.reciprocal(rstd[:, 32 + t:33 + t], root[:, 32 + t:33 + t]).then_inc(s_rs2, 1)
                    v.wait_ge(s_rs2, t + 1)
                    if t >= 2:
                        v.wait_ge(s_sh[b], 16 * (t // 2))
                    v.scalar_tensor_tensor(h2[:, b, :], x1[:, b, :], rstd[:, 32 + t:33 + t], rows3[:, SF, :],
                                           ALU.mult, ALU.mult).then_inc(s_ha, 1)
                normed(NT - 1)

            @block.tensor
            def _(pe):
                for i in range(4):
                    pe.wait_ge(s_dg3, i + 1)
                    if i >= 2:
                        pe.wait_ge(s_r3, i - 1)
                    for h in range(2):
                        mm = pe.matmul(PS[:, (i % 2) * 2 + h, :], ones[:], diag3[:, i % 2, 4 * h:4 * h + 4, :], start=True, stop=True)
                    mm.then_inc(s_b3, 1)
                pe.wait_ge(s_r3, 4)

                def mixed(t):
                    pe.wait_ge(s_mx, 2 * t + 2)
                    for h in range(2):
                        if t:
                            pe.wait_ge(s_tml, 2 * (t - 1) + h + 1)
                        for q in range(4):
                            mm = pe.transpose(PS[:, h, q * P:(q + 1) * P], mx[:, t % 2, (4 * h + q) * P:(4 * h + q + 1) * P], ident[:])
                        mm.then_inc(s_tm, 1)

                def normed(t):
                    b = t % 2
                    pe.wait_ge(s_h2, t + 1)
                    for h in range(2):
                        if t:
                            pe.wait_ge(s_thl, 2 * (t - 1) + h + 1)
                        for q in range(4):
                            mm = pe.transpose(PS[:, 4 + h, q * P:(q + 1) * P], h2[:, b, (4 * h + q) * P:(4 * h + q + 1) * P], ident[:])
                        mm.then_inc(s_th, 1)
                    pe.wait_ge(s_thh, 2 * t + 2)
                    pe.wait_ge(s_thl, 2 * t + 2)
                    n = 0
                    for dc in range(DC):
                        for ht, wt in ((gTh, wrh), (gTh, wrl), (gTl, wrh)):
                            mm = pe.matmul(PS[:, 6, t * N_EXPERTS:(t + 1) * N_EXPERTS], ht[:, b, dc, :], wt[:, dc, :],
                                           start=(n == 0), stop=(n == 3 * DC - 1))
                            n += 1
                    mm.then_inc(s_lg, 1)

                mixed(0)
                for t in range(NT):
                    b = t % 2
                    if t + 1 < NT:
                        mixed(t + 1)
                    pe.wait_ge(s_tmh, 2 * t + 2)
                    pe.wait_ge(s_tml, 2 * t + 2)
                    pe.wait_ge(s_wol, DC)
                    if t:
                        pe.wait_ge(s_xa, t)
                    for h in range(2):
                        n = 0
                        for dc in range(DC):
                            for mt, wt in ((mTh, woh), (mTh, wol), (mTl, woh)):
                                mm = pe.matmul(PS[:, 2 + h, :], mt[:, b, dc, :], wt[:, dc, h * HALF:(h + 1) * HALF],
                                               start=(n == 0), stop=(n == 3 * DC - 1))
                                n += 1
                    mm.then_inc(s_wp3, 1)
                    if t:
                        if t == 1:
                            pe.wait_ge(s_wrl, 1)
                        normed(t - 1)
                normed(NT - 1)

        biasr = at("bias_row", AT, [P, N_EXPERTS], F32)
        sel = at("sel", AT + 0.25, [P, NT, N_EXPERTS], F32)
        top2 = at("top2", AT + 2.25, [P, NT * N_GROUPS, 8], F32)
        gsum = at("gsum", AT + 4.25, [P, NT, N_GROUPS], F32)
        cmp1 = at("cmp1", AT + 4.5, [P, NT, N_GROUPS, N_GROUPS], F32)
        cmp2 = at("cmp2", AT + 6.5, [P, NT, N_GROUPS, N_GROUPS], F32)
        before = at("before", AT + 8.5, [P, N_GROUPS, N_GROUPS], F32)
        grank = at("grank", AT + 8.75, [P, NT * N_GROUPS], F32)
        gpen = at("gpen", AT + 9, [P, NT * N_GROUPS], F32)
        selm = at("selm", AT + 9.25, [P, NT, N_EXPERTS], F32)
        top8 = at("top8", AT + 11.25, [P, NT, 8], F32)
        repl = at("repl", AT + 11.5, [P, NT, N_EXPERTS], F32)
        mask = at("mask", AT + 13.5, [P, NT, N_EXPERTS], F32)
        maskb = at("maskb", AT + 15.5, [P, NT, N_EXPERTS], BF16)
        wts = at("wts", AT + 16.5, [P, NT, N_EXPERTS], F32)
        wsum = at("wsum", AT + 18.5, [P, 4, NT], F32)
        utri = at("utri", AT + 19, [P, P], BF16)
        onesb = at("onesb", AT + 19.25, [P, P], BF16)
        utrif = at("utrif", AT + 19.5, [P, P], F32)
        erow = at("erow", AT + 20, [P, 12, N_EXPERTS], F32)
        erowi = at("erowi", AT + 23, [P, 2, N_EXPERTS], I32)
        pos = at("pos", AT + 23.5, [P, NT, N_EXPERTS], F32)
        pos8 = at("pos8", AT + 25.5, [P, NT, 8], F32)
        posi = at("posi", AT + 25.75, [P, 3, NT * 8], I32)
        blk8 = at("blk8", AT + 26.5, [P, NT * 8], F32)
        slt8 = at("slt8", AT + 26.75, [P, NT * 8], F32)
        w8 = at("w8", AT + 27, [P, NT * 8], F32)
        ojunk = at("ojunk", AT + 64, [P, NT * TOP_K + 1, N_EXPERTS], F32)
        ioti = at("iota_i", AT + 27.5, [P, P], I32)
        iotf = at("iota_f", AT + 28, [P, P], F32)
        tokf = at("tok1_f", AT + 28.5, [P, 16], F32)
        toki = at("tok1_i", AT + 28.5625, [P, 16], I32)
        NB4 = 4
        onea = at("onehot_slot", AT + 29, [P, NB4, P], F32)
        oneb = at("onehot_block", AT + 31, [P, NB4, 2, P], F32)
        tabf = at("tab_f", AT + 35, [P, 4, P], F32)
        rcol = at("rcol", AT + 37, [P, 8], F32)
        rowf = at("rowf", AT + 38, [P, 3, TAB], F32)
        zero_t = at("zero_t", AT + 40, [P, D], F32)

        s_ri = sem("s_ri")
        s_rk = sem("s_rk")
        s_bl = sem("s_bl")
        s_mb = sem("s_mb")
        s_cm = sem("s_cm")
        s_oa = sem("s_oa")
        s_ob = sem("s_ob")
        s_tb = sem("s_tb")
        s_s8 = sem("s_s8")
        s_rc2 = sem("s_rc2")
        s_rt4 = sem("s_rt4")
        s_zt = sem("s_zt")
        s_zd = sem("s_zd")
        PAIRS = [(t, k) for t in range(NT) for k in range(TOP_K)]
        (NBK, PEND, PSTA, ACTV, CACT, PBASE, ONE, CNT) = range(8)

        with nc.Block() as block:
            @block.sync
            def _(sp):
                sp.dma_start(biasr[:], router_bias.broadcast_to([P, N_EXPERTS])).then_inc(s_bl, 16)
                sp.wait_ge(s_zt, 1)
                sp.dma_start(acc_dram[T:T + P, :], zero_t[:]).then_inc(s_zd, 16)
                sp.wait_ge(s_zd, 16)

            @block.gpsimd
            def _(po):
                po.memset(utrif[:], 1.0).then_inc(s_ri, 1)
                po.memset(before[:], 1.0).then_inc(s_ri, 1)
                po.memset(onesb[:], 1.0).then_inc(s_ri, 1)
                po.iota(ioti[:], [[1, P]], base=0, channel_multiplier=0).then_inc(s_ri, 1)
                po.iota(toki[:, 0:NT], [[P, NT]], base=1, channel_multiplier=1).then_inc(s_ri, 1)
                po.wait_ge(s_ri, 5)
                po.affine_select(out=utrif[:], in_=utrif[:], compare_op=ALU.is_gt, fill=0.0, base=0,
                                 pattern=[[1, P]], channel_multiplier=-1).then_inc(s_ri, 1)
                po.affine_select(out=before[:], in_=before[:], compare_op=ALU.is_gt, fill=0.0, base=0,
                                 pattern=[[1, N_GROUPS], [-1, N_GROUPS]], channel_multiplier=0).then_inc(s_ri, 1)
                po.tensor_copy(iotf[:], ioti[:]).then_inc(s_ri, 1)
                po.tensor_copy(tokf[:, 0:NT], toki[:, 0:NT]).then_inc(s_ri, 1)
                po.wait_ge(s_ri, 9)
                po.tensor_copy(utri[:], utrif[:]).then_inc(s_ri, 1)
                po.memset(zero_t[:], 0.0).then_inc(s_zt, 1)
                po.memset(gidx[:], SKIP).then_inc(s_ri, 1)
                po.memset(sidx[:], 0).then_inc(s_ri, 1)
                po.memset(wtab[:], 0.0).then_inc(s_ri, 1)
                po.memset(btab[0:1], 0).then_inc(s_ri, 1)
                po.memset(erow[:, ONE, :], 1.0).then_inc(s_ri, 1)
                po.memset(rowf[0:1], 0.0).then_inc(s_ri, 1)
                po.wait_ge(s_s8, 1)
                for n in range(len(PAIRS)):
                    if n >= NB4:
                        po.wait_ge(s_tb, n - NB4 + 1)
                    po.tensor_scalar(onea[:, n % NB4, :], iotf[:], slt8[:, n:n + 1], None, ALU.is_equal).then_inc(s_oa, 1)

            @block.vector
            def _(v):
                n = [0]

                def link(ins):
                    n[0] += 1
                    ins.then_inc(s_rk, 1)
                    v.wait_ge(s_rk, n[0])

                def step(ins):
                    n[0] += 1
                    ins.then_inc(s_rk, 1)

                v.wait_ge(s_bl, 16)
                v.wait_ge(s_ri, 16)
                link(v.tensor_tensor(sel[:], score_t[:], biasr[:, None, :].broadcast_to([P, NT, N_EXPERTS]), ALU.add))
                for t in range(NT):
                    for g in range(N_GROUPS):
                        step(v.max(out=top2[:, t * N_GROUPS + g, :], in_=sel[:, t, g * PER_GROUP:(g + 1) * PER_GROUP]))
                v.wait_ge(s_rk, n[0])
                gs = gsum[:].rearrange("p t g -> p (t g)")
                link(v.tensor_tensor(gs, top2[:, :, 0], top2[:, :, 1], ALU.add))
                mine = gsum[:, :, :, None].broadcast_to([P, NT, N_GROUPS, N_GROUPS])
                other = gsum[:, :, None, :].broadcast_to([P, NT, N_GROUPS, N_GROUPS])
                step(v.tensor_tensor(cmp1[:], other, mine, ALU.is_gt))
                link(v.tensor_tensor(cmp2[:], other, mine, ALU.is_equal))
                c2 = cmp2[:].rearrange("p t g j -> p t (g j)")
                bf = before[:].rearrange("p g j -> p (g j)")
                link(v.tensor_tensor(c2, c2, bf[:, None, :].broadcast_to([P, NT, 64]), ALU.mult))
                link(v.tensor_tensor(cmp1[:], cmp1[:], cmp2[:], ALU.add))
                link(v.tensor_reduce(grank[:], cmp1[:].rearrange("p t g j -> p (t g) j"), AX, ALU.add))
                link(v.tensor_scalar(gpen[:], grank[:], float(TOP_GROUPS), BIG, ALU.is_lt, ALU.mult))
                link(v.tensor_scalar(gpen[:], gpen[:], BIG, None, ALU.subtract))
                link(v.tensor_tensor(selm[:].rearrange("p t (g e) -> p (t g) e", g=N_GROUPS),
                                     sel[:].rearrange("p t (g e) -> p (t g) e", g=N_GROUPS),
                                     gpen[:, :, None].broadcast_to([P, NT * N_GROUPS, PER_GROUP]), ALU.add))
                for t in range(NT):
                    step(v.max(out=top8[:, t, :], in_=selm[:, t, :]))
                v.wait_ge(s_rk, n[0])
                for t in range(NT):
                    step(v.match_replace(out=repl[:, t, :], in_to_replace=top8[:, t, :], in_values=selm[:, t, :], imm_value=LOWEST))
                v.wait_ge(s_rk, n[0])
                link(v.tensor_tensor(mask[:], repl[:], selm[:], ALU.not_equal))
                v.tensor_copy(maskb[:], mask[:]).then_inc(s_mb, 1)
                link(v.tensor_tensor(wts[:], score_t[:], mask[:], ALU.mult))
                link(v.tensor_reduce(wsum[:, 0, :], wts[:], AX, ALU.add))
                link(v.reciprocal(wsum[:, 1, :], wsum[:, 0, :]))
                link(v.tensor_scalar(wsum[:, 2, :], wsum[:, 1, :], ROUTED_SCALE, None, ALU.mult))
                link(v.tensor_tensor(wts[:], wts[:], wsum[:, 2, :][:, :, None].broadcast_to([P, NT, N_EXPERTS]), ALU.mult))
                v.wait_ge(s_cm, 1)
                link(v.tensor_scalar(erowi[:, 0, :], PS[:, 1, 0:N_EXPERTS], float(P - 1), None, ALU.add))
                link(v.tensor_scalar(erowi[:, 1, :], erowi[:, 0, :], 7, None, ALU.arith_shift_right))
                link(v.tensor_copy(erow[:, NBK, :], erowi[:, 1, :]))
                link(v.tensor_tensor_scan(erow[:, PEND, :], erow[:, ONE, :], erow[:, NBK, :], 0.0, ALU.mult, ALU.add))
                link(v.tensor_tensor(erow[:, PSTA, :], erow[:, PEND, :], erow[:, NBK, :], ALU.subtract))
                link(v.tensor_scalar(erow[:, ACTV, :], erow[:, NBK, :], 0.0, None, ALU.is_gt))
                link(v.tensor_tensor_scan(erow[:, CACT, :], erow[:, ONE, :], erow[:, ACTV, :], 0.0, ALU.mult, ALU.add))
                link(v.tensor_scalar(erow[:, PBASE, :], erow[:, PSTA, :], float(P), 1.0, ALU.mult, ALU.add))
                link(v.tensor_tensor(pos[:], PS[:, 0, :].rearrange("p (t e) -> p t e", t=NT),
                                     erow[:, PBASE, :][:, None, :].broadcast_to([P, NT, N_EXPERTS]), ALU.add))
                link(v.tensor_tensor(pos[:], pos[:], mask[:], ALU.mult))
                link(v.tensor_scalar(pos[:], pos[:], -1.0, None, ALU.add))
                for t in range(NT):
                    step(v.max(out=pos8[:, t, :], in_=pos[:, t, :]))
                v.wait_ge(s_rk, n[0])
                link(v.tensor_copy(posi[:, 0, :], pos8[:].rearrange("p t k -> p (t k)")))
                step(v.tensor_scalar(posi[:, 1, :], posi[:, 0, :], 7, None, ALU.arith_shift_right))
                link(v.tensor_scalar(posi[:, 2, :], posi[:, 0, :], P - 1, None, ALU.bitwise_and))
                step(v.tensor_copy(blk8[:], posi[:, 1, :]))
                v.tensor_copy(slt8[:], posi[:, 2, :]).then_inc(s_s8, 1)
                for i, (t, k) in enumerate(PAIRS):
                    step(v.scalar_tensor_tensor(ojunk[:, i, :], pos[:, t, :], pos8[:, t, k:k + 1], wts[:, t, :],
                                                ALU.is_equal, ALU.mult, accum_out=w8[:, i:i + 1]))
                v.wait_ge(s_rk, n[0])
                for i, (t, k) in enumerate(PAIRS):
                    if i >= NB4:
                        v.wait_ge(s_tb, i - NB4 + 1)
                    v.tensor_scalar(oneb[:, i % NB4, 0, :], iotf[:], blk8[:, i:i + 1], tokf[:, t:t + 1], ALU.is_equal, ALU.mult).then_inc(s_ob, 1)
                    v.tensor_scalar(oneb[:, i % NB4, 1, :], iotf[:], blk8[:, i:i + 1], w8[:, i:i + 1], ALU.is_equal, ALU.mult).then_inc(s_ob, 1)
                v.wait_ge(s_tb, len(PAIRS))
                tok = PS[:, 2, 0:P]
                step(v.tensor_copy(wtab[:, 0:P], PS[:, 2, P:2 * P]))
                step(v.tensor_scalar(tabf[:, 0, :], tok, 0.0, None, ALU.is_equal))
                step(v.tensor_scalar(tabf[:, 1, :], tok, -1.0, None, ALU.add))
                link(v.tensor_scalar(rcol[:, 0:1], tokf[:, 0:1], float(T), None, ALU.add))
                step(v.scalar_tensor_tensor(gidx[:, 0:P], tabf[:, 0, :], float(SKIP), tabf[:, 1, :], ALU.mult, ALU.add))
                step(v.scalar_tensor_tensor(sidx[:, 0:P], tabf[:, 0, :], rcol[:, 0:1], tabf[:, 1, :], ALU.mult, ALU.add))
                link(v.tensor_scalar(rcol[:, 1:2], tokf[:, 0:1], -1.0, None, ALU.add))
                step(v.scalar_tensor_tensor(ojunk[:, NT * TOP_K, :], erow[:, PSTA, :], rcol[:, 1:2], erow[:, ACTV, :],
                                            ALU.is_le, ALU.mult, accum_out=rcol[:, 2:3]))
                step(v.scalar_tensor_tensor(tabf[:, 2, 0:N_EXPERTS], erow[:, CACT, :], rcol[:, 1:2], erow[:, ONE, :],
                                            ALU.is_le, ALU.mult, accum_out=rcol[:, 3:4]))
                v.wait_ge(s_rk, n[0])
                v.engine_nop().then_inc(s_rc2, 1)
                v.wait_ge(s_rt4, 1)
                step(v.tensor_copy(rowf[0:1, 0, 1:P + 1], PS[0:1, 3, 0:P]))
                link(v.tensor_scalar(rowf[0:1, 1, 0:P], PS[0:1, 3, P:2 * P], float(N_EXPERTS - 1), None, ALU.min))
                step(v.tensor_copy(btab[0:1, 0, 0:P], rowf[0:1, 0, 1:P + 1]))
                step(v.tensor_tensor(btab[0:1, 1, 0:P], rowf[0:1, 0, 1:P + 1], rowf[0:1, 0, 0:P], ALU.subtract))
                link(v.tensor_copy(etab[0:1, 0:P], rowf[0:1, 1, 0:P]))
                step(v.tensor_scalar(btab[0:1, 2, 0:P], btab[0:1, 0, 0:P], 1, None, ALU.bitwise_and))
                step(v.tensor_scalar(btab[0:1, 4, 0:P], btab[0:1, 0, 0:P], 1, None, ALU.arith_shift_right))
                step(v.tensor_scalar(btab[0:1, 5, 0:1], erow[0:1, CACT, N_EXPERTS - 1:N_EXPERTS], 1.0, None, ALU.add))
                link(v.tensor_scalar(btab[0:1, 5, 1:2], erow[0:1, PEND, N_EXPERTS - 1:N_EXPERTS], 1.0, None, ALU.add))
                step(v.tensor_tensor(btab[0:1, 3, 0:P], btab[0:1, 4, 0:P], btab[0:1, 2, 0:P], ALU.add))
                link(v.tensor_scalar(btab[0:1, 5, 2:4], btab[0:1, 5, 0:2], 1, 1, ALU.arith_shift_right, ALU.arith_shift_left))

            @block.tensor
            def _(pe):
                pe.wait_ge(s_ri, 10)
                pe.wait_ge(s_mb, 1)
                for t in range(NT):
                    for u in range(t + 1):
                        mm = pe.matmul(PS[:, 0, t * N_EXPERTS:(t + 1) * N_EXPERTS], (utri if u == t else onesb)[:], maskb[:, u, :],
                                       start=(u == 0), stop=(u == t))
                for u in range(NT):
                    mm = pe.matmul(PS[:, 1, 0:N_EXPERTS], onesb[:], maskb[:, u, :], start=(u == 0), stop=(u == NT - 1))
                mm.then_inc(s_cm, 1)
                for i in range(len(PAIRS)):
                    pe.wait_ge(s_oa, i + 1)
                    pe.wait_ge(s_ob, 2 * i + 2)
                    pe.matmul(PS[:, 2, 0:2 * P], onea[:, i % NB4, :], oneb[:, i % NB4].rearrange("p a b -> p (a b)"),
                              start=(i == 0), stop=(i == len(PAIRS) - 1)).then_inc(s_tb, 1)
                pe.wait_ge(s_rc2, 1)
                pe.matmul(PS[0:1, 3, 0:P], rcol[:, 2:3], ident[:], start=True, stop=True)
                pe.matmul(PS[0:1, 3, P:2 * P], rcol[:, 3:4], ident[:], start=True, stop=True).then_inc(s_rt4, 1)

        eraw = at("eraw", AT, [P, 2, 3, UNIT], F32)
        eh = at("e_hi", AT + 48, [P, 2, 3, UNIT], F32R)
        el = at("e_lo", AT + 96, [P, 2, 3, UNIT], F32R)
        xg = [at("xgA", AT + 144, [P, D], F32), at("xgB", AT + 148, [P, D], F32)]
        xh = [at("xhA", AT + 152, [P, DC, P], F32R), at("xhB", AT + 156, [P, DC, P], F32R)]
        xl = [at("xlA", AT + 160, [P, DC, P], F32R), at("xlB", AT + 164, [P, DC, P], F32R)]
        yb = [at("ybA", AT + 168, [P, D], F32), at("ybB", AT + 172, [P, D], F32)]
        sg = [at("sgA", AT + 176, [P, F], F32), at("sgB", AT + 177, [P, F], F32)]
        ga = [at("gaA", AT + 178, [P, F], F32), at("gaB", AT + 179, [P, F], F32)]
        ah = [at("ahA", AT + 180, [P, FC, P], F32R), at("ahB", AT + 181, [P, FC, P], F32R)]
        al = [at("alA", AT + 182, [P, FC, P], F32R), at("alB", AT + 183, [P, FC, P], F32R)]
        GU0, XT0, AT0, Y0 = 0, 2, (4, 7), 5

        e_sh = sem("e_shared_loaded")
        e_gu = [sem("e_gate_up_even"), sem("e_gate_up_odd")]
        e_dn = [sem("e_down_even"), sem("e_down_odd")]
        e_hgu = sem("e_gate_up_hi")
        e_lgu = sem("e_gate_up_lo")
        e_hd = sem("e_down_hi")
        e_ld = sem("e_down_lo")
        e_g = [sem("e_gathered_a"), sem("e_gathered_b")]
        e_x = sem("e_x_transposed")
        e_xh = sem("e_x_hi")
        e_xl = sem("e_x_lo")
        e_p = sem("e_gate_up_done")
        e_s = sem("e_sigmoid")
        e_w = sem("e_weighted")
        e_a = sem("e_act")
        e_t = sem("e_act_transposed")
        e_ah = sem("e_act_hi")
        e_al = sem("e_act_lo")
        e_y = sem("e_down_done")
        e_ya = sem("e_y_low_half")
        e_yd = sem("e_y_high_half")
        e_o = [sem("e_added_a"), sem("e_added_b")]
        e_ig = sem("e_gather_indices")
        e_is = sem("e_scatter_indices")
        SHB = NT

        wg_v = w_gate[0].rearrange("e (p c) n -> e p (c n)", p=P)
        wu_v = w_up[0].rearrange("e (p c) n -> e p (c n)", p=P)
        wd_v = w_down[0].rearrange("e (p c) n -> e p (c n)", p=P)

        def entry(eng, row, b, hi):
            return eng.value_load(btab[0:1, row, bass.ds(b, 1)], min_val=0, max_val=hi)

        def n_blocks(eng):
            return eng.value_load(btab[0:1, 5, 3:4], min_val=2, max_val=P)

        def gu_view(w, slot):
            return w[:, slot, 0:2, :].rearrange("p g (c n) -> p g c n", c=DC)

        with nc.Block() as block:
            @block.sync
            def _(sp):
                sp.sem_inc(e_gu[0], 32)
                sp.sem_inc(e_dn[0], 16)
                sp.dma_start(eraw[:, 0, 0, :], ws_gate[0].rearrange("(p c) n -> p (c n)", p=P)).then_inc(e_sh, 16)
                sp.dma_start(eraw[:, 0, 1, :], ws_up[0].rearrange("(p c) n -> p (c n)", p=P)).then_inc(e_sh, 16)
                sp.dma_start(eraw[:, 0, 2, :], ws_down[0].rearrange("(p c) n -> p (c n)", p=P)).then_inc(e_sh, 16)

                def load(slot, e):
                    for k, w in enumerate((wg_v, wu_v)):
                        sp.dma_start(eraw[:, slot, k, :], w[bass.ds(e, 1)].rearrange("e p n -> p (e n)")).then_inc(e_gu[slot], 16)
                    sp.dma_start(eraw[:, slot, 2, :], wd_v[bass.ds(e, 1)].rearrange("e p n -> p (e n)")).then_inc(e_dn[slot], 16)

                def expert(r):
                    return sp.value_load(etab[0:1, bass.ds(r - 1, 1)], min_val=0, max_val=N_EXPERTS - 1)

                used = sp.value_load(btab[0:1, 5, 2:3], min_val=TOP_K, max_val=N_EXPERTS)
                load(1, sp.value_load(etab[0:1, 0:1], min_val=0, max_val=N_EXPERTS - 1))
                sp.wait_ge(e_hgu, 1)
                sp.wait_ge(e_lgu, 1)
                sp.wait_ge(e_hd, 1)
                sp.wait_ge(e_ld, 1)
                load(0, sp.value_load(etab[0:1, 1:2], min_val=0, max_val=N_EXPERTS - 1))
                with sp.Fori(3, used + 1, 2) as r:
                    for j in range(2):
                        for s in (e_hgu, e_lgu, e_hd, e_ld):
                            sp.wait_ge(s, r + j - 1)
                        load(1 - j, expert(r + j))

            @block.gpsimd
            def _(po):
                def fetch_shared(j, G):
                    po.wait_ge(e_x, G * 2 + 2 * j + 2)
                    po.dma_start(xg[j][:], h2_dram[bass.ds((G + 2 + j) * P, P), :]).then_inc(e_g[j], 16)

                def fetch_routed(j, G, b):
                    po.wait_ge(e_x, G * 2 + 2 * j + 2)
                    po.tensor_copy(gnow[:, j, 0:1], gidx[:, bass.ds(b, 1)]).then_inc(e_ig, 2)
                    po.wait_ge(s_sh[j], 16)
                    po.wait_ge(e_ig, G * 2 + 2 * j + 2)
                    po.indirect_dma_start(xg[j][:], None, h2_dram[:, :], bass.IndirectOffsetOnAxis(ap=gnow[:, j, 0:1], axis=0),
                                          bounds_check=T - 1, oob_is_err=False).then_inc(e_g[j], 16)

                def results(G, b):
                    for j in range(2):
                        if b is None:
                            po.wait_ge(e_ya, G + j + 2)
                            po.wait_ge(e_yd, G + j + 2)
                            po.dma_start(acc_dram[bass.ds((G + j) * P, P), :], yb[j][:]).then_inc(e_o[j], 16)
                        else:
                            po.wait_ge(e_o[1 - j], G * 8 + 16 * j)
                            po.wait_ge(e_ya, G + j + 2)
                            po.tensor_copy(snow[:, j, 0:1], sidx[:, bass.ds(b + j, 1)]).then_inc(e_is, 1)
                            po.wait_ge(s_zd, 16)
                            po.wait_ge(e_is, G + j + 2)
                            po.wait_ge(e_yd, G + j + 2)
                            po.indirect_dma_start(acc_dram[:, :], bass.IndirectOffsetOnAxis(ap=snow[:, j, 0:1], axis=0), yb[j][:], None,
                                                  compute_op=ALU.add).then_inc(e_o[j], 16)

                po.sem_inc(e_ig, 2 * (SHB - 2))
                po.sem_inc(e_is, SHB + 1)
                for j in range(2):
                    po.dma_start(xg[j][:], h2_dram[j * P:(j + 1) * P, :]).then_inc(e_g[j], 16)
                with po.Fori(0, SHB - 3, 2) as G:
                    for j in range(2):
                        fetch_shared(j, G)
                    results(G, None)
                for j in range(2):
                    fetch_routed(j, SHB - 2, j)
                results(SHB - 2, None)
                with po.Fori(0, n_blocks(po), 2) as b:
                    for j in range(2):
                        fetch_routed(j, b + SHB, b + 2 + j)
                    results(b + SHB, b)
                used = po.value_load(btab[0:1, 5, 2:3], min_val=TOP_K, max_val=N_EXPERTS)
                n = n_blocks(po)
                for i in range(2):
                    po.wait_ge(e_gu[i], used * 16 + 32 * (1 - i))
                    po.wait_ge(e_dn[i], used * 8 + 16 * (1 - i))
                for j in range(2):
                    po.wait_ge(e_g[j], n * 8 + 16 * (SHB // 2 + 1))
                    po.wait_ge(e_o[j], n * 8 + 16 * (SHB // 2))

            def split_engine(eng, high):
                gu_done, dn_done = (e_hgu, e_hd) if high else (e_lgu, e_ld)

                def part(dst, src, other, done):
                    if high:
                        return eng.copy(dst, src)
                    return eng.tensor_tensor(dst, src, other.bitcast(F32), ALU.subtract)

                def slots(k0, k1, slot):
                    if isinstance(slot, int):
                        return tuple(w[:, slot, k0:k1, :] for w in (eh, eraw, el))
                    return tuple(w[:, bass.ds(slot, 1), k0:k1, :].rearrange("p s k n -> p (s k) n") for w in (eh, eraw, el))

                def gate_up(slot, rank):
                    hi, src, lo = slots(0, 2, slot)
                    if not high:
                        eng.wait_ge(e_hgu, rank + 1)
                    part(hi if high else lo, src, hi, gu_done).then_inc(gu_done, 1)

                def down(slot, rank):
                    hi, src, lo = slots(2, 3, slot)
                    if not high:
                        eng.wait_ge(e_hd, rank + 1)
                    part(hi if high else lo, src, hi, dn_done).then_inc(dn_done, 1)

                def new_gate_up(b, guard, first):
                    fresh = entry(eng, 1, b, 1)
                    with eng.If(fresh):
                        rank = entry(eng, 0, b, N_EXPERTS)
                        slot = entry(eng, 2, b, 1)
                        eng.wait_ge(e_gu[1], entry(eng, 3, b, 64) * 32)
                        eng.wait_ge(e_gu[0], entry(eng, 4, b, 64) * 32 + 32)
                        eng.wait_ge(e_p, guard)
                        gate_up(slot, rank)

                def new_down(b, guard):
                    fresh = entry(eng, 1, b, 1)
                    with eng.If(fresh):
                        rank = entry(eng, 0, b, N_EXPERTS)
                        slot = entry(eng, 2, b, 1)
                        eng.wait_ge(e_dn[1], entry(eng, 3, b, 64) * 16)
                        eng.wait_ge(e_dn[0], entry(eng, 4, b, 64) * 16 + 16)
                        eng.wait_ge(e_y, guard)
                        down(slot, rank)

                return gate_up, down, new_gate_up, new_down

            def quads_of(bank):
                return PS[:, bank, :].rearrange("p (c m) -> p c m", c=4)

            @block.scalar
            def _(act):
                gate_up, down, new_gate_up, new_down = split_engine(act, True)

                def sigmoid(j, X):
                    act.wait_ge(e_p, X + 1)
                    act.activation(sg[j][:], PS[:, GU0 + j, 0:F], ACT.Sigmoid).then_inc(e_s, 1)

                def x_high(j, X):
                    for h in range(2):
                        act.wait_ge(e_x, X * 2 + h + 1)
                        act.copy(xh[j][:, 4 * h:4 * h + 4, :], quads_of(XT0 + h)).then_inc(e_xh, 1)

                def act_high(j, X):
                    act.wait_ge(e_t, X + 1)
                    act.copy(ah[j][:], PS[:, AT0[j], 0:F].rearrange("p (c m) -> p c m", c=FC)).then_inc(e_ah, 1)

                def y_low(j, X, G):
                    act.wait_ge(e_y, X * 2 + 1)
                    if not (isinstance(G, int) and G == 0):
                        act.wait_ge(e_o[j], G * 8)
                    act.copy(yb[j][:, 0:HALF], PS[:, Y0, :]).then_inc(e_ya, 1)

                def pair(G, b, ahead):
                    if b is not None:
                        new_gate_up(b + 1, G, False)
                        new_down(b, G * 2)
                    sigmoid(0, G)
                    if b is not None:
                        new_down(b + 1, G * 2)
                        new_gate_up(b + 2, G + 1, False)
                    sigmoid(1, G + 1)
                    act_high(0, G)
                    if ahead:
                        x_high(0, G + 2)
                    y_low(0, G, G)
                    if ahead:
                        x_high(1, G + 3)
                    act_high(1, G + 1)
                    y_low(1, G + 1, G)

                act.sem_inc(e_ya, 1)
                act.wait_ge(e_sh, 48)
                gate_up(0, 0)
                down(0, 0)
                x_high(0, 0)
                x_high(1, 1)
                pair(0, None, True)
                with act.Fori(2, SHB - 3, 2) as G:
                    pair(G, None, True)
                act.wait_ge(e_gu[1], 32)
                gate_up(1, 1)
                pair(SHB - 2, None, False)
                x_high(0, SHB)
                x_high(1, SHB + 1)
                with act.Fori(0, n_blocks(act), 2) as b:
                    pair(b + SHB, b, True)

            @block.vector
            def _(v):
                gate_up, down, new_gate_up, new_down = split_engine(v, False)

                def gated(j, X, b):
                    v.wait_ge(e_s, X + 1)
                    w = 1.0 if b is None else wtab[:, bass.ds(b, 1)]
                    v.scalar_tensor_tensor(ga[j][:], PS[:, GU0 + j, 0:F], w, sg[j][:], ALU.mult, ALU.mult).then_inc(e_w, 1)
                    v.wait_ge(e_w, X + 1)
                    v.tensor_tensor(ga[j][:], ga[j][:], PS[:, GU0 + j, F:2 * F], ALU.mult).then_inc(e_a, 1)

                def x_low(j, X):
                    for h in range(2):
                        v.wait_ge(e_xh, X * 2 + h + 1)
                        v.tensor_tensor(xl[j][:, 4 * h:4 * h + 4, :], quads_of(XT0 + h), xh[j][:, 4 * h:4 * h + 4, :].bitcast(F32),
                                        ALU.subtract).then_inc(e_xl, 1)

                def act_low(j, X):
                    v.wait_ge(e_ah, X + 1)
                    v.tensor_tensor(al[j][:], PS[:, AT0[j], 0:F].rearrange("p (c m) -> p c m", c=FC), ah[j][:].bitcast(F32),
                                    ALU.subtract).then_inc(e_al, 1)

                def y_high(j, X, G):
                    v.wait_ge(e_y, X * 2 + 2)
                    if not (isinstance(G, int) and G == 0):
                        v.wait_ge(e_o[j], G * 8)
                    v.tensor_copy(yb[j][:, HALF:D], PS[:, Y0 + 1, :]).then_inc(e_yd, 1)

                def pair(G, b, ahead):
                    if b is not None:
                        new_gate_up(b + 1, G, False)
                        new_down(b, G * 2)
                    gated(0, G, b)
                    if b is not None:
                        new_down(b + 1, G * 2)
                        new_gate_up(b + 2, G + 1, False)
                    gated(1, G + 1, None if b is None else b + 1)
                    act_low(0, G)
                    if ahead:
                        x_low(0, G + 2)
                    y_high(0, G, G)
                    if ahead:
                        x_low(1, G + 3)
                    act_low(1, G + 1)
                    y_high(1, G + 1, G)

                v.sem_inc(e_yd, 1)
                v.wait_ge(e_sh, 48)
                gate_up(0, 0)
                down(0, 0)
                x_low(0, 0)
                x_low(1, 1)
                pair(0, None, True)
                with v.Fori(2, SHB - 3, 2) as G:
                    pair(G, None, True)
                gate_up(1, 1)
                pair(SHB - 2, None, False)
                x_low(0, SHB)
                x_low(1, SHB + 1)
                with v.Fori(0, n_blocks(v), 2) as b:
                    pair(b + SHB, b, True)

            @block.tensor
            def _(pe):
                def gate_up(j, X, rank, slot):
                    pe.wait_ge(e_xh, X * 2 + 2)
                    pe.wait_ge(e_xl, X * 2 + 2)
                    pe.wait_ge(e_hgu, rank + 1)
                    pe.wait_ge(e_lgu, rank + 1)
                    n = 0
                    for dc in range(DC):
                        for xp, wp in ((xh, eh), (xl, eh), (xh, el)):
                            if isinstance(slot, int):
                                w = wp[:, slot, 0:2, dc * F:(dc + 1) * F]
                            else:
                                w = wp[:, bass.ds(slot, 1), 0:2, dc * F:(dc + 1) * F].rearrange("p s k n -> p (s k) n")
                            mm = pe.matmul(PS[:, GU0 + j, :], xp[j][:, dc, :], w, start=(n == 0), stop=(n == 3 * DC - 1))
                            n += 1
                    mm.then_inc(e_p, 1)

                def x_transposed(j, X, gathered, guard):
                    pe.wait_ge(e_g[j], gathered)
                    rows = xg[j][:].rearrange("p (m c) -> p c m", c=DC)
                    for h in range(2):
                        if guard is not None:
                            pe.wait_ge(e_xl, guard + h + 1)
                        for q in range(4):
                            mm = pe.transpose(PS[:, XT0 + h, q * P:(q + 1) * P], rows[:, 4 * h + q, :], ident[:])
                        mm.then_inc(e_x, 1)

                def act_transposed(j, X):
                    pe.wait_ge(e_a, X + 1)
                    cols = ga[j][:].rearrange("p (m c) -> p c m", c=FC)
                    for fc in range(FC):
                        mm = pe.transpose(PS[:, AT0[j], fc * P:(fc + 1) * P], cols[:, fc, :], ident[:])
                    mm.then_inc(e_t, 1)

                def down(j, X, h, rank, slot):
                    if h == 0:
                        pe.wait_ge(e_ah, X + 1)
                        pe.wait_ge(e_al, X + 1)
                        pe.wait_ge(e_hd, rank + 1)
                        pe.wait_ge(e_ld, rank + 1)
                    pe.wait_ge(e_yd if h else e_ya, X + 1)
                    n = 0
                    for fc in range(FC):
                        for ap, wp in ((ah, eh), (al, eh), (ah, el)):
                            c0 = fc * D + h * HALF
                            if isinstance(slot, int):
                                w = wp[:, slot, 2, c0:c0 + HALF]
                            else:
                                w = wp[:, bass.ds(slot, 1), 2, c0:c0 + HALF].rearrange("p s n -> p (s n)")
                            mm = pe.matmul(PS[:, Y0 + h, :], ap[j][:, fc, :], w, start=(n == 0), stop=(n == 3 * FC - 1))
                            n += 1
                    mm.then_inc(e_y, 1)

                def pair(G, b, ahead):
                    if b is None:
                        rs = [(0, 0), (0, 0)]
                    else:
                        rs = [(entry(pe, 0, b + j, N_EXPERTS), entry(pe, 2, b + j, 1)) for j in range(2)]
                    gate_up(0, G, *rs[0])
                    gate_up(1, G + 1, *rs[1])
                    act_transposed(0, G)
                    if ahead:
                        x_transposed(0, G + 2, G * 8 + 32, G * 2 + 2)
                    down(0, G, 0, *rs[0])
                    if ahead:
                        x_transposed(1, G + 3, G * 8 + 32, G * 2 + 4)
                    act_transposed(1, G + 1)
                    down(0, G, 1, *rs[0])
                    down(1, G + 1, 0, *rs[1])
                    down(1, G + 1, 1, *rs[1])

                x_transposed(0, 0, 16, None)
                x_transposed(1, 1, 16, 0)
                pair(0, None, True)
                with pe.Fori(2, SHB - 3, 2) as G:
                    pair(G, None, True)
                pair(SHB - 2, None, False)
                x_transposed(0, SHB, 8 * SHB + 16, 2 * SHB - 2)
                x_transposed(1, SHB + 1, 8 * SHB + 16, 2 * SHB)
                with pe.Fori(0, n_blocks(pe), 2) as b:
                    pair(b + SHB, b, True)

        ff = at("ff", AT, [P, NT, D], F32)
        xf = at("xf", AT + 32, [P, NT, D], F32)
        of = at("of", AT + 64, [P, NT, D], F32)
        rowg = at("rowg", AT + 96, [P, D], F32)
        diagf = at("diagf", AT + 100, [P, DC, P], F32)
        fj = at("fj", AT + 104, [P, D], F32)
        f_l = s_x
        f_x = sem("f_x")
        f_q = sem("f_q")
        f_r = sem("f_r")
        f_v = sem("f_v")
        f_d = sem("f_d")
        f_b = sem("f_b")
        f_g = sem("f_g")
        f_m = sem("f_m")
        f_o = sem("f_o")
        f_s = sem("f_s")

        with nc.Block() as block:
            @block.sync
            def _(sp):
                for t in range(NT):
                    sp.dma_start(ff[:, t, :], acc_dram[t * P:(t + 1) * P, :]).then_inc(f_l[t], 16)
                for t in range(NT):
                    sp.wait_ge(f_o, t + 1)
                    sp.dma_start(out[0, t * P:(t + 1) * P, :], of[:, t, :]).then_inc(f_s, 16)
                sp.wait_ge(f_s, 16 * NT)

            @block.gpsimd
            def _(po):
                for t in range(NT):
                    po.wait_ge(f_m, t + 1)
                    po.wait_ge(f_x, 16 * NT)
                    po.tensor_tensor(of[:, t, :], of[:, t, :], xf[:, t, :], ALU.add).then_inc(f_o, 1)

            @block.scalar
            def _(act):
                for t in range(NT):
                    act.dma_start(xf[:, t, :], x1_dram[t * P:(t + 1) * P, :]).then_inc(f_x, 16)
                for t in range(NT):
                    act.wait_ge(f_l[t], 32)
                    act.activation(fj[:], ff[:, t, :], ACT.Square, accum_out=ssum[:, 32 + t:33 + t]).then_inc(f_q, 1)
                    act.wait_ge(f_q, t + 1)
                    act.activation(root[:, 40 + t:41 + t], ssum[:, 32 + t:33 + t], ACT.Sqrt, bias=epsc[:, 0:1], scale=1.0 / D).then_inc(f_r, 1)

            @block.vector
            def _(v):
                v.tensor_tensor(diagf[:], ident[:, None, :].broadcast_to([P, DC, P]),
                                vecc[:, 3, :][:, :, None].broadcast_to([P, DC, P]), ALU.mult).then_inc(f_d, 1)
                v.wait_ge(f_b, 1)
                v.tensor_copy(rowg[:], flat2(0)).then_inc(f_g, 1)
                v.wait_ge(f_g, 1)
                for t in range(NT):
                    v.wait_ge(f_r, t + 1)
                    v.reciprocal(rstd[:, 40 + t:41 + t], root[:, 40 + t:41 + t]).then_inc(f_v, 1)
                    v.wait_ge(f_v, t + 1)
                    v.scalar_tensor_tensor(of[:, t, :], ff[:, t, :], rstd[:, 40 + t:41 + t], rowg[:], ALU.mult, ALU.mult).then_inc(f_m, 1)

            @block.tensor
            def _(pe):
                pe.wait_ge(f_d, 1)
                for h in range(2):
                    mm = pe.matmul(PS[:, h, :], ones[:], diagf[:, 4 * h:4 * h + 4, :], start=True, stop=True)
                mm.then_inc(f_b, 1)


_INS = ['x', 'c', 'w_ada', 'b_ada', 'g_pre_mix', 'g_post_mix', 'g_pre_ffn', 'g_post_ffn', 'w_in', 'b_forget',
        'w_pool', 'pool_scale', 'g_pool_out', 'g_attn_out', 'w_out', 'w_router', 'router_bias',
        'w_gate', 'w_up', 'w_down', 'ws_gate', 'ws_up', 'ws_down']


def kernel(**inputs):
    import numpy as np
    import concourse.bacc as bacc
    from concourse.bass_utils import run_bass_kernel_spmd

    nc = bacc.Bacc("TRN2", target_bir_lowering=False, num_devices=1)
    arrays, args = {}, []
    for name in _INS:
        a = np.ascontiguousarray(inputs[name])
        arrays[f"in_{name}"] = a
        args.append(nc.dram_tensor(f"in_{name}", a.shape, mybir.dt.from_np(a.dtype), kind="ExternalInput").ap())
    args.append(nc.dram_tensor("out_0", (1, T, D), F32, kind="ExternalOutput").ap())
    args.append(nc.dram_tensor("x1_dram", (T, D), F32, kind="Internal").ap())
    args.append(nc.dram_tensor("h2_dram", (T, D), F32, kind="Internal").ap())
    args.append(nc.dram_tensor("acc_dram", (T + P, D), F32, kind="Internal").ap())
    build(nc, *args)
    r = run_bass_kernel_spmd(nc, [arrays], core_ids=[0])
    return r.results[0]["out_0"]
```

```python
from contextlib import ExitStack

import concourse.bass as bass
from concourse import mybir

F32 = mybir.dt.float32
F32R = mybir.dt.float32r
BF16 = mybir.dt.bfloat16
I32 = mybir.dt.int32
ALU = mybir.AluOpType
ACT = mybir.ActivationFunctionType
AX = mybir.AxisListType.X

P = 128
D = 1024
T = 1024
NT = T // P
DC = D // P
HALF = 512
D_POOL = 512
N_HEADS = 8
DH = 64
WINDOWS = (2, 4, 8, 16)
NG = len(WINDOWS)
N_EXPERTS = 64
N_GROUPS = 8
PER_GROUP = N_EXPERTS // N_GROUPS
TOP_GROUPS = 4
TOP_K = 8
F = 256
FC = F // P
ROUTED_SCALE = 2.5
EPS = 1e-6
UNIT = 2048
UC = 256
TAB = P + 4
SKIP = 5000
LOWEST = -3.0e38
BIG = 1.0e30

C_C, C_ADA, C_GPM, C_GOM, C_GPF, C_GOF, C_PS, C_GMIX = 0, 8, 56, 64, 72, 80, 88, 92
N_PARAM = 100

BASE = 16512
KB = 1024
AT = 11


def build(nc, x, c, w_ada, b_ada, g_pre_mix, g_post_mix, g_pre_ffn, g_post_ffn, w_in, b_forget,
          w_pool, pool_scale, g_pool_out, g_attn_out, w_out, w_router, router_bias,
          w_gate, w_up, w_down, ws_gate, ws_up, ws_down, out, x1_dram, h2_dram, acc_dram):
    stack = ExitStack()

    def sem(name):
        return stack.enter_context(nc.semaphore(name))

    def at(name, kb, shape, dt):
        return nc.alloc_sbuf_tensor_at(name, shape, dt, offset=BASE + int(kb * KB))

    with stack:
        PS = stack.enter_context(nc.psum_tensor("PS", [P, 8, HALF], F32))

        ident = at("ident", 0, [P, P], F32)
        ones = at("ones", 0.5, [P, P], F32)
        pcol = at("pcol", 1, [P, P], F32)
        modc = at("modc", 1.5, [P, 48], F32)
        vecc = at("vecc", 1.75, [P, 6, DC], F32)
        epsc = at("epsc", 2, [P, 8], F32)
        ssum = at("ssum", 2.0625, [P, 64], F32)
        root = at("root", 2.3125, [P, 64], F32)
        rstd = at("rstd", 2.5625, [P, 64], F32)
        mmax = at("mmax", 2.8125, [P, 128], F32)
        negm = at("negm", 3.3125, [P, 64], F32)
        psum_row = at("prob_sum", 3.5625, [P, 64], F32)
        prec = at("prob_rec", 3.8125, [P, 64], F32)
        gidx = at("gather_rows", 4.0625, [P, TAB], I32)
        sidx = at("scatter_rows", 4.625, [P, TAB], I32)
        wtab = at("slot_weight", 5.1875, [P, TAB], F32)
        btab = at("block_table", 5.75, [P, 6, TAB], I32)
        etab = at("expert_table", 8.875, [P, TAB + 4], I32)
        bfc = at("b_forget_col", 9.4375, [P, 8], F32)
        gnow = at("gather_now", 9.5, [P, 2, 8], I32)
        snow = at("scatter_now", 9.5625, [P, 2, 8], I32)

        uqkv = at("uqkv", AT, [P, 16384], F32)
        hTh = at("hT_hi", AT + 64, [P, DC, T], F32R)
        hTl = at("hT_lo", AT + 96, [P, DC, T], F32R)
        wsh = at("w_hi", AT + 128, [P, 2, DC, P], F32R)
        wsl = at("w_lo", AT + 136, [P, 2, DC, P], F32R)
        vT = at("vT", AT + 144, [P, T], F32)
        NR = 4
        raw = at("raw", AT + 148, [P, NR, UNIT], F32)
        zf = at("zf", AT + 180, [P, T], F32)
        prow = at("prow", AT + 184, [P, P], F32)
        uT = uqkv[:, 0:4096].rearrange("p (g t) -> p g t", g=4)
        qT = uqkv[:, 4096:8192].rearrange("p (g t) -> p g t", g=4)
        kT = uqkv[:, 8192:12288].rearrange("p (g t) -> p g t", g=4)
        vr = uqkv[:, 12288:16384].rearrange("p (t f) -> p t f", t=NT)
        xin = uqkv[:, 8192:16384].rearrange("p (t d) -> p t d", t=NT)
        row_sm = uqkv[:, 0:D]
        row_bm = uqkv[:, D:2 * D]
        diag = [uqkv[:, 2048:3072].rearrange("p (c m) -> p c m", c=DC),
                uqkv[:, 3072:4096].rearrange("p (c m) -> p c m", c=DC)]
        wf = at("wf", AT + 188, [P, DC, P], F32)

        units = [("ada", u) for u in range(8)] + [("win", u) for u in range(8)] \
            + [("ada", u) for u in range(8, 24)]
        unit_at = {key: n for n, key in enumerate(units)}

        s_const = sem("s_const")
        s_prow = sem("s_prow")
        s_x = [sem(f"s_x_tile{t}") for t in range(NT)]
        s_raw = [sem(f"s_raw{i}") for i in range(NR)]
        s_wf0 = sem("s_wf0")
        s_wf = sem("s_wf")
        s_pt = sem("s_pt")
        s_pcol = sem("s_pcol")
        s_ada = sem("s_ada")
        s_ss = sem("s_ss")
        s_rt = sem("s_rt")
        s_rs = sem("s_rs")
        s_mod = sem("s_mod")
        s_diag = sem("s_diag")
        s_bc = sem("s_bc")
        s_row = sem("s_row")
        s_hx = sem("s_hx")
        s_h = sem("s_h")
        s_tr = sem("s_tr")
        s_hh = sem("s_hh")
        s_hl = sem("s_hl")
        s_wh = sem("s_wh")
        s_wl = sem("s_wl")
        s_pj = sem("s_pj")
        s_eva = sem("s_eva")
        s_evd = sem("s_evd")
        s_vt = sem("s_vt")
        s_va = sem("s_va")
        s_vd = sem("s_vd")
        s_bf = sem("s_bf")

        def raw_wait(eng, key):
            n = unit_at[key]
            eng.wait_ge(s_raw[n % NR], 16 * (n // NR + 1))
            return raw[:, n % NR, :]

        with nc.Block() as block:
            @block.sync
            def _(sp):
                rows = [(c.rearrange("b (r m) -> (b r) m", m=P), 8), (b_ada.rearrange("l (r m) -> (l r) m", m=P), 48)]
                rows += [(g.rearrange("l (r m) -> (l r) m", m=P), 8)
                         for g in (g_pre_mix, g_post_mix, g_pre_ffn, g_post_ffn)]
                rows += [(g.rearrange("l (r m) -> (l r) m", m=P), 4) for g in (pool_scale, g_pool_out, g_attn_out)]
                r0 = 0
                for src, n in rows:
                    sp.dma_start(prow[r0:r0 + n, :], src).then_inc(s_prow, 16)
                    r0 += n
                sp.dma_start(bfc[0:8, 0:1], b_forget.rearrange("l h -> h l")).then_inc(s_bf, 16)
                for n, (kind, u) in enumerate(units):
                    if n >= NR:
                        k, v = units[n - NR]
                        if k == "ada":
                            sp.wait_ge(s_ada, v + 1)
                        else:
                            sp.wait_ge(s_wh, 2 * v + 2)
                            sp.wait_ge(s_wl, 2 * v + 2)
                    w = w_ada if kind == "ada" else w_in
                    sp.dma_start(raw[:, n % NR, :].rearrange("p (c n) -> p c n", c=DC),
                                 w[0, :, u * UC:(u + 1) * UC].rearrange("(c p) n -> p c n", p=P)
                                 ).then_inc(s_raw[n % NR], 16)
                sp.wait_ge(s_bf, 16)

            @block.gpsimd
            def _(po):
                po.memset(ident[:], 0.0).then_inc(s_const, 1)
                po.memset(ones[:], 1.0).then_inc(s_const, 1)
                po.memset(epsc[:], EPS).then_inc(s_const, 1)
                po.wait_ge(s_const, 1)
                po.affine_select(out=ident[:], in_=ident[:], compare_op=ALU.not_equal, fill=1.0, base=0,
                                 pattern=[[-1, P]], channel_multiplier=1).then_inc(s_const, 1)
                po.memset(wf[:], 0.0).then_inc(s_wf0, 1)
                po.wait_ge(s_wf0, 1)
                po.dma_start(wf[:, :, 0:8], w_in[0, :, 2048:2056].rearrange("(c p) n -> p c n", p=P)).then_inc(s_wf, 16)
                po.wait_ge(s_row, 4)
                for t in range(NT):
                    po.wait_ge(s_hx, t + 1)
                    po.tensor_tensor(xin[:, t, :], xin[:, t, :], row_bm, ALU.add).then_inc(s_h, 1)
                po.wait_ge(s_wf, 16)

            @block.scalar
            def _(act):
                for t in range(NT):
                    act.dma_start(xin[:, t, :], x[0, t * P:(t + 1) * P, :]).then_inc(s_x[t], 16)
                act.wait_ge(s_const, 4)
                for t in range(NT):
                    act.wait_ge(s_x[t], 16)
                    if t:
                        act.wait_ge(s_ss, t)
                    act.activation(PS[:, 5:7, :].rearrange("p a b -> p (a b)"), xin[:, t, :], ACT.Square,
                                   accum_out=ssum[:, t:t + 1]).then_inc(s_ss, 1)
                act.wait_ge(s_ss, NT)
                act.activation(root[:, 0:NT], ssum[:, 0:NT], ACT.Sqrt, bias=epsc[:, 0:1], scale=1.0 / D).then_inc(s_rt, 1)
                act.wait_ge(s_bc, 2)
                act.copy(row_bm, PS[:, 2:4, :].rearrange("p a b -> p (a b)")).then_inc(s_row, 2)

                def split(f):
                    if f < 16:
                        src = raw_wait(act, ("win", f // 2)).rearrange("p (c n) -> p c n", c=DC)[:, :, (f % 2) * P:(f % 2 + 1) * P]
                    else:
                        src = wf[:]
                        act.wait_ge(s_wf, 16)
                    if f >= 2:
                        act.wait_ge(s_pj, 2 * (f - 1))
                    act.copy(wsh[:, f % 2], src).then_inc(s_wh, 1)

                for t in range(NT):
                    for h in range(2):
                        act.wait_ge(s_tr, 2 * t + h + 1)
                        act.copy(hTh[:, 4 * h:4 * h + 4, t * P:(t + 1) * P],
                                 PS[:, (t % 2) * 2 + h, :].rearrange("p (c m) -> p c m", c=4)).then_inc(s_hh, 1)
                    if t < 2:
                        split(t)
                for f in range(17):
                    if f + 1 < 17 and f >= 1:
                        split(f + 1)
                    act.wait_ge(s_pj, 2 * f + 1)
                    src = PS[:, (f % 2) * 2, :]
                    if f < 12:
                        if 4 <= f < 8:
                            act.mul(uqkv[:, f * T:f * T + HALF], src, DH ** -0.5).then_inc(s_eva, 1)
                        else:
                            act.copy(uqkv[:, f * T:f * T + HALF], src).then_inc(s_eva, 1)
                    elif f < 16:
                        if f > 12:
                            act.wait_ge(s_vt, f - 12)
                        act.copy(vT[:, 0:HALF], src).then_inc(s_eva, 1)
                    else:
                        act.copy(zf[0:8, 0:HALF], src[0:8, :]).then_inc(s_eva, 1)
                    if 12 < f <= 16:
                        fc = f - 13
                        act.wait_ge(s_vt, fc + 1)
                        act.copy(vr[:, 0:4, fc * P:(fc + 1) * P], PS[:, 4, :].rearrange("p (t m) -> p t m", t=4)).then_inc(s_va, 1)

            @block.vector
            def _(v):
                v.wait_ge(s_pt, 1)
                v.tensor_copy(pcol[:, 0:N_PARAM], PS[:, 7, 0:N_PARAM]).then_inc(s_pcol, 1)
                v.wait_ge(s_rt, 1)
                v.reciprocal(rstd[:, 0:NT], root[:, 0:NT]).then_inc(s_rs, 1)
                v.wait_ge(s_ada, 8)
                v.wait_ge(s_pcol, 1)
                v.tensor_tensor(modc[:, 0:16], PS[:, 7, P:P + 16], pcol[:, C_ADA:C_ADA + 16], ALU.add).then_inc(s_mod, 1)
                v.wait_ge(s_mod, 1)
                v.scalar_tensor_tensor(vecc[:, 0, :], modc[:, 8:16], 1.0, pcol[:, C_GPM:C_GPM + 8],
                                       ALU.add, ALU.mult).then_inc(s_mod, 1)
                v.wait_ge(s_mod, 2)
                v.wait_ge(s_const, 4)
                for i, col in enumerate((vecc[:, 0, :], modc[:, 0:8])):
                    v.tensor_tensor(diag[i], ident[:, None, :].broadcast_to([P, DC, P]),
                                    col[:, :, None].broadcast_to([P, DC, P]), ALU.mult).then_inc(s_diag, 1)
                v.wait_ge(s_bc, 1)
                v.tensor_copy(row_sm, PS[:, 0:2, :].rearrange("p a b -> p (a b)")).then_inc(s_row, 2)
                v.wait_ge(s_row, 4)
                v.wait_ge(s_rs, 1)
                for t in range(NT):
                    v.scalar_tensor_tensor(xin[:, t, :], xin[:, t, :], rstd[:, t:t + 1], row_sm,
                                           ALU.mult, ALU.mult).then_inc(s_hx, 1)

                def split(f):
                    if f < 16:
                        src = raw_wait(v, ("win", f // 2)).rearrange("p (c n) -> p c n", c=DC)[:, :, (f % 2) * P:(f % 2 + 1) * P]
                    else:
                        src = wf[:]
                        v.wait_ge(s_wf, 16)
                    v.wait_ge(s_wh, f + 1)
                    if f >= 2:
                        v.wait_ge(s_pj, 2 * (f - 1))
                    v.tensor_tensor(wsl[:, f % 2], src, wsh[:, f % 2].bitcast(F32), ALU.subtract).then_inc(s_wl, 1)

                for t in range(NT):
                    for h in range(2):
                        v.wait_ge(s_hh, 2 * t + h + 1)
                        dst = (slice(None), slice(4 * h, 4 * h + 4), slice(t * P, (t + 1) * P))
                        v.tensor_tensor(hTl[dst], PS[:, (t % 2) * 2 + h, :].rearrange("p (c m) -> p c m", c=4),
                                        hTh[dst].bitcast(F32), ALU.subtract).then_inc(s_hl, 1)
                    if t < 2:
                        split(t)
                for f in range(17):
                    if f + 1 < 17 and f >= 1:
                        split(f + 1)
                    v.wait_ge(s_pj, 2 * f + 2)
                    src = PS[:, (f % 2) * 2 + 1, :]
                    if f < 12:
                        if 4 <= f < 8:
                            v.tensor_scalar(uqkv[:, f * T + HALF:(f + 1) * T], src, DH ** -0.5, None, ALU.mult).then_inc(s_evd, 1)
                        else:
                            v.tensor_copy(uqkv[:, f * T + HALF:(f + 1) * T], src).then_inc(s_evd, 1)
                    elif f < 16:
                        if f > 12:
                            v.wait_ge(s_vt, f - 12)
                        v.tensor_copy(vT[:, HALF:T], src).then_inc(s_evd, 1)
                    else:
                        v.tensor_copy(zf[0:8, HALF:T], src[0:8, :]).then_inc(s_evd, 1)
                    if 12 < f <= 16:
                        fc = f - 13
                        v.wait_ge(s_vt, fc + 1)
                        v.tensor_copy(vr[:, 4:8, fc * P:(fc + 1) * P], PS[:, 5, :].rearrange("p (t m) -> p t m", t=4)).then_inc(s_vd, 1)
                v.wait_ge(s_ada, 24)
                v.tensor_tensor(modc[:, 16:48], PS[:, 7, P + 16:P + 48], pcol[:, C_ADA + 16:C_ADA + 48], ALU.add).then_inc(s_mod, 1)
                v.wait_ge(s_mod, 3)
                v.tensor_tensor(vecc[:, 1, :], modc[:, 16:24], pcol[:, C_GOM:C_GOM + 8], ALU.mult).then_inc(s_mod, 1)
                v.scalar_tensor_tensor(vecc[:, 2, :], modc[:, 32:40], 1.0, pcol[:, C_GPF:C_GPF + 8],
                                       ALU.add, ALU.mult).then_inc(s_mod, 1)
                v.tensor_tensor(vecc[:, 3, :], modc[:, 40:48], pcol[:, C_GOF:C_GOF + 8], ALU.mult).then_inc(s_mod, 1)
                v.wait_ge(s_mod, 6)

            @block.tensor
            def _(pe):
                def gemv(u):
                    w = raw_wait(pe, ("ada", u)).rearrange("p (c n) -> p c n", c=DC)
                    for fc in range(2):
                        for dc in range(DC):
                            mm = pe.matmul(PS[:, 7, P + 2 * u + fc:P + 2 * u + fc + 1], w[:, dc, fc * P:(fc + 1) * P],
                                           pcol[:, C_C + dc:C_C + dc + 1], start=(dc == 0), stop=(dc == DC - 1))
                    mm.then_inc(s_ada, 1)

                pe.wait_ge(s_const, 4)
                pe.wait_ge(s_prow, 144)
                pe.transpose(PS[:, 7, 0:N_PARAM], prow[0:N_PARAM, :], ident[0:N_PARAM, 0:N_PARAM]).then_inc(s_pt, 1)
                pe.wait_ge(s_pcol, 1)
                for u in range(8):
                    gemv(u)
                for i in range(2):
                    pe.wait_ge(s_diag, i + 1)
                    for h in range(2):
                        mm = pe.matmul(PS[:, 2 * i + h, :], ones[:], diag[i][:, 4 * h:4 * h + 4, :], start=True, stop=True)
                    mm.then_inc(s_bc, 1)
                for t in range(NT):
                    pe.wait_ge(s_h, t + 1)
                    for h in range(2):
                        if t >= 2:
                            pe.wait_ge(s_hl, 2 * (t - 2) + h + 1)
                        for q in range(4):
                            dc = 4 * h + q
                            mm = pe.transpose(PS[:, (t % 2) * 2 + h, q * P:(q + 1) * P], xin[:, t, dc * P:(dc + 1) * P], ident[:])
                        mm.then_inc(s_tr, 1)
                pe.wait_ge(s_hl, 2 * NT)

                def v_transposes(fc):
                    pe.wait_ge(s_eva, 13 + fc)
                    pe.wait_ge(s_evd, 13 + fc)
                    if fc:
                        pe.wait_ge(s_va, fc)
                        pe.wait_ge(s_vd, fc)
                    for t in range(NT):
                        mm = pe.transpose(PS[:, 4 + t // 4, (t % 4) * P:(t % 4 + 1) * P], vT[:, t * P:(t + 1) * P], ident[:])
                    mm.then_inc(s_vt, 1)

                for f in range(17):
                    pe.wait_ge(s_wh, f + 1)
                    pe.wait_ge(s_wl, f + 1)
                    if f >= 2:
                        pe.wait_ge(s_eva, f - 1)
                        pe.wait_ge(s_evd, f - 1)
                    if 12 < f <= 16:
                        v_transposes(f - 13)
                    for h in range(2):
                        n = 0
                        for dc in range(DC):
                            for wt, ht in ((wsh, hTh), (wsh, hTl), (wsl, hTh)):
                                mm = pe.matmul(PS[:, (f % 2) * 2 + h, :], wt[:, f % 2, dc, :], ht[:, dc, h * HALF:(h + 1) * HALF],
                                               start=(n == 0), stop=(n == 3 * DC - 1))
                                n += 1
                        mm.then_inc(s_pj, 1)
                for u in range(8, 24):
                    gemv(u)

        ymix = at("ymix", AT + 64, [P, NT, D], F32)
        woraw = at("woraw", AT + 96, [P, DC, D], F32)
        psrow = at("psrow", AT + 128, [P, D_POOL], F32)
        nckb = at("nckb", AT + 130, [P, 2, T], F32)
        nckd = at("nckd", AT + 138, [P, 2, T], F32)
        Sb = at("Sb", AT + 146, [P, 2, T], F32)
        Pm = at("Pm", AT + 154, [P, 2, T], F32)
        PT = at("PT", AT + 162, [P, 2, NT, P], F32)
        pw = [at("pwA", AT + 170, [P, T], F32), at("pwB", AT + 174, [P, T], F32)]
        wpl = at("wpl", AT + 178, [P, NG, P], F32)
        cum = zf
        sel8 = at("sel8", AT + 184, [P, N_HEADS, P], F32)
        lz = at("lz", AT + 188, [P, 2, T], F32)
        diag4 = at("diag4", AT + 188, [P, 4, P], F32)
        counti = at("counti", 9.75, [P, 16], I32)
        countf = at("countf", 9.8125, [P, 16], F32)
        rinv = at("rinv", 9.875, [P, 16], F32)

        s_c2 = sem("s_c2")
        s_wo = sem("s_wo")
        s_wp = sem("s_wp")
        s_lf = sem("s_lf")
        s_la = sem("s_la")
        s_cum = sem("s_cum")
        s_nk = sem("s_nk")
        s_nb = sem("s_nb")
        s_nd = sem("s_nd")
        s_s = sem("s_s")
        s_t1 = sem("s_t1")
        s_t2 = sem("s_t2")
        s_ng = sem("s_ng")
        s_ex = sem("s_ex")
        s_pT = sem("s_pT")
        s_pta = sem("s_pta")
        s_ptd = sem("s_ptd")
        s_pv = sem("s_pv")
        s_rc = sem("s_rc")
        s_rr = sem("s_rr")
        s_oe = sem("s_oe")
        s_pw = sem("s_pw")
        s_po = sem("s_po")
        s_yp = sem("s_yp")
        s_ye = sem("s_ye")
        s_dg2 = sem("s_dg2")
        s_b2 = sem("s_b2")
        s_r2 = sem("s_r2")
        s_sm = sem("s_sm")
        s_md = sem("s_md")

        steps = [(h, q) for h in range(N_HEADS) for q in range(NT)]
        NS = len(steps)

        def taken(i, act):
            return (i + 1) // 2 if act else (i + 2) // 2

        with nc.Block() as block:
            @block.sync
            def _(sp):
                sp.dma_start(wpl[:], w_pool[0].rearrange("g c d -> c g d")).then_inc(s_wp, 16)
                for q in range(4):
                    sp.dma_start(woraw[:, 2 * q:2 * q + 2, :],
                                 w_out[0, 2 * q * P:(2 * q + 2) * P, :].rearrange("(c p) n -> p c n", p=P)).then_inc(s_wo, 16)
                sp.wait_ge(s_wp, 16)
                sp.wait_ge(s_wo, 64)

            @block.gpsimd
            def _(po):
                po.memset(sel8[0:8], 0.0).then_inc(s_c2, 1)
                po.wait_ge(s_c2, 1)
                po.affine_select(out=sel8[0:8], in_=sel8[0:8], compare_op=ALU.not_equal, fill=-1.0, base=0,
                                 pattern=[[-1, N_HEADS], [0, P]], channel_multiplier=1).then_inc(s_c2, 1)
                po.iota(counti[:], [[1, 16]], base=1, channel_multiplier=0).then_inc(s_c2, 1)
                done = [0]

                def link(ins):
                    done[0] += 1
                    ins.then_inc(s_pw, 1)
                    po.wait_ge(s_pw, done[0])

                def diagonal(h):
                    if h >= 2:
                        po.wait_ge(s_t1, 8 * (h - 1))
                    po.wait_ge(s_nb, 2 * h + 2)
                    po.affine_select(out=nckd[:, h % 2, :].rearrange("p (q m) -> p q m", q=NT),
                                     in_=nckb[:, h % 2, :].rearrange("p (q m) -> p q m", q=NT),
                                     compare_op=ALU.is_ge, fill=-BIG, base=0,
                                     pattern=[[0, NT], [-1, P]], channel_multiplier=1).then_inc(s_nd, 1)

                po.wait_ge(s_rr, 1)
                for g, w in enumerate(WINDOWS):
                    diagonal(g)
                    cur = uT[:, g, :]
                    s, k = 1, 0
                    while s < w:
                        nxt = pw[k % 2]
                        link(po.tensor_copy(nxt[:, 0:s], cur[:, 0:s]))
                        link(po.tensor_tensor(nxt[:, s:T], cur[:, s:T], cur[:, 0:T - s], ALU.add))
                        cur = nxt
                        s, k = 2 * s, k + 1
                    nxt = pw[k % 2]
                    link(po.tensor_scalar(nxt[:, w:T], cur[:, w:T], 1.0 / w, None, ALU.mult))
                    link(po.tensor_tensor(nxt[:, 0:w], cur[:, 0:w], rinv[:, 0:w], ALU.mult))
                    link(po.tensor_tensor(uT[:, g, :], nxt[:], uT[:, g, :], ALU.subtract))
                po.sem_inc(s_po, 1)
                for h in range(NG, N_HEADS):
                    diagonal(h)

            @block.scalar
            def _(act):
                act.wait_ge(s_lf, 3)
                act.activation(lz[0:8, 0, :], lz[0:8, 0, :], ACT.Exp, scale=-1.0).then_inc(s_la, 1)
                act.wait_ge(s_la, 1)
                act.activation(lz[0:8, 0, :], lz[0:8, 0, :], ACT.Ln, bias=1.0).then_inc(s_la, 1)

                def key_term(n):
                    h, half = divmod(n, 2)
                    if h >= 2:
                        act.wait_ge(s_t2, 8 * (h - 1))
                        act.wait_ge(s_nd, h - 1)
                    act.wait_ge(s_nk, n + 1)
                    act.copy(nckb[:, h % 2, half * HALF:(half + 1) * HALF], PS[:, 6, :]).then_inc(s_nb, 1)

                def transposed(i):
                    act.wait_ge(s_pT, i + 1)
                    q = steps[i][1]
                    if i >= 2:
                        act.wait_ge(s_pv, i - 1)
                    act.copy(PT[:, i % 2, 0:q + 1, :], PS[:, 4:6, :].rearrange("p a (b m) -> p (a b) m", m=P)[:, 0:q + 1, :]).then_inc(s_pta, 1)

                key_term(0)
                key_term(1)
                for i, (h, q) in enumerate(steps):
                    act.wait_ge(s_ng, i + 1)
                    if i >= 2:
                        act.wait_ge(s_pT, i - 1)
                    w = (q + 1) * P
                    act.activation(Pm[:, i % 2, 0:w], Sb[:, i % 2, 0:w], ACT.Exp, bias=negm[:, i:i + 1],
                                   accum_out=psum_row[:, i:i + 1]).then_inc(s_ex, 1)
                    if i >= 1 and (i - 1) % 2 == 1:
                        transposed(i - 1)
                    if h + 1 < N_HEADS and q in (4, 6):
                        key_term(2 * (h + 1) + (q - 4) // 2)
                transposed(NS - 1)
                for t in range(NT):
                    act.wait_ge(s_oe, 8 * 7 + t + 1)
                    if t:
                        act.wait_ge(s_sm, 2 * t)
                    act.activation(Pm[:, 0, 0:HALF], ymix[:, t, HALF:D], ACT.Square, accum_out=ssum[:, 8 + t:9 + t]).then_inc(s_sm, 1)
                    act.wait_ge(s_ye, t + 1)
                    act.activation(Pm[:, 1, 0:HALF], ymix[:, t, 0:HALF], ACT.Square, accum_out=ssum[:, t:t + 1]).then_inc(s_sm, 1)

            @block.vector
            def _(v):
                v.wait_ge(s_c2, 3)
                v.tensor_copy(countf[:], counti[:]).then_inc(s_md, 1)
                v.wait_ge(s_md, 1)
                v.reciprocal(rinv[:], countf[:]).then_inc(s_rr, 1)
                v.tensor_scalar(zf[0:8, :], zf[0:8, :], bfc[0:8, 0:1], None, ALU.add).then_inc(s_lf, 1)
                v.wait_ge(s_lf, 1)
                v.scalar_tensor_tensor(lz[0:8, 0, :], zf[0:8, :], -1.0, zf[0:8, :], ALU.mult, ALU.max).then_inc(s_lf, 1)
                v.tensor_scalar(lz[0:8, 1, :], zf[0:8, :], 0.0, None, ALU.min).then_inc(s_lf, 1)
                v.wait_ge(s_la, 2)
                v.wait_ge(s_lf, 3)
                v.tensor_tensor(lz[0:8, 1, :], lz[0:8, 1, :], lz[0:8, 0, :], ALU.subtract).then_inc(s_lf, 1)
                v.wait_ge(s_lf, 4)
                v.memset(lz[0:8, 0, :], 1.0).then_inc(s_lf, 1)
                v.wait_ge(s_lf, 5)
                v.tensor_tensor_scan(cum[0:8, :], lz[0:8, 0, :], lz[0:8, 1, :], 0.0, ALU.mult, ALU.add).then_inc(s_cum, 1)
                v.wait_ge(s_cum, 1)
                v.tensor_tensor(diag4[:], ident[:, None, :].broadcast_to([P, 4, P]),
                                pcol[:, C_PS:C_PS + 4][:, :, None].broadcast_to([P, 4, P]), ALU.mult).then_inc(s_dg2, 1)
                v.wait_ge(s_b2, 1)
                v.tensor_copy(psrow[:], PS[:, 5, :]).then_inc(s_r2, 1)

                def score(i):
                    h, q = steps[i]
                    v.wait_ge(s_s, i + 1)
                    v.wait_ge(s_nd, h + 1)
                    if i >= 2:
                        v.wait_ge(s_ex, i - 1)
                    flat = PS[:, (i % 2) * 2:(i % 2) * 2 + 2, :].rearrange("p a b -> p (a b)")
                    w = q * P
                    first = v.tensor_tensor_reduce(Sb[:, i % 2, w:w + P], flat[:, w:w + P], nckd[:, h % 2, w:w + P], 1.0, LOWEST,
                                                   ALU.add, ALU.max, mmax[:, 2 * (i % 32):2 * (i % 32) + 1])
                    first.then_inc(s_t1, 1)
                    v.wait_ge(s_t1, i + 1)
                    col = 2 * (i % 32)
                    if q:
                        v.tensor_tensor_reduce(Sb[:, i % 2, 0:w], flat[:, 0:w], nckb[:, h % 2, 0:w], 1.0, mmax[:, col:col + 1],
                                               ALU.add, ALU.max, mmax[:, col + 1:col + 2]).then_inc(s_t2, 1)
                        col += 1
                    else:
                        v.engine_nop().then_inc(s_t2, 1)
                    v.wait_ge(s_t2, i + 1)
                    v.tensor_scalar(negm[:, i:i + 1], mmax[:, col:col + 1], -1.0, None, ALU.mult).then_inc(s_ng, 1)

                def transposed(i):
                    v.wait_ge(s_pT, i + 1)
                    q = steps[i][1]
                    if i >= 2:
                        v.wait_ge(s_pv, i - 1)
                    v.tensor_copy(PT[:, i % 2, 0:q + 1, :], PS[:, 4:6, :].rearrange("p a (b m) -> p (a b) m", m=P)[:, 0:q + 1, :]).then_inc(s_ptd, 1)

                def output(i):
                    h, q = steps[i]
                    v.wait_ge(s_ex, i + 1)
                    v.reciprocal(prec[:, i:i + 1], psum_row[:, i:i + 1]).then_inc(s_rc, 1)
                    v.wait_ge(s_rc, i + 1)
                    v.wait_ge(s_pv, i + 1)
                    v.tensor_scalar(ymix[:, q, HALF + h * DH:HALF + (h + 1) * DH], PS[:, 7 - i % 2, 0:DH],
                                    prec[:, i:i + 1], None, ALU.mult).then_inc(s_oe, 1)

                score(0)
                for i in range(NS):
                    if i + 1 < NS:
                        score(i + 1)
                    if i % 2 == 0:
                        transposed(i)
                    if i >= 2:
                        output(i - 2)
                output(NS - 2)
                output(NS - 1)
                for t in range(NT):
                    v.wait_ge(s_yp, t + 1)
                    v.tensor_tensor(ymix[:, t, 0:HALF], PS[:, t % 2, :], psrow[:], ALU.mult).then_inc(s_ye, 1)

            @block.tensor
            def _(pe):
                pe.wait_ge(s_dg2, 1)
                pe.matmul(PS[:, 5, :], ones[:], diag4[:], start=True, stop=True).then_inc(s_b2, 1)
                pe.wait_ge(s_r2, 1)

                key_terms = [0]

                def key_term(n):
                    h, half = divmod(n, 2)
                    if n:
                        pe.wait_ge(s_nb, n)
                    key_terms[0] = n + 1
                    pe.matmul(PS[:, 6, :], sel8[0:8, h, :], cum[0:8, half * HALF:(half + 1) * HALF], start=True, stop=True).then_inc(s_nk, 1)

                def score(i):
                    h, q = steps[i]
                    if i >= 2:
                        pe.wait_ge(s_t1, i - 1)
                        pe.wait_ge(s_t2, i - 1)
                    pb = (h % 2) * DH
                    w = (q + 1) * P
                    for k0 in range(0, w, HALF):
                        n = min(HALF, w - k0)
                        mm = pe.matmul(PS[:, (i % 2) * 2 + k0 // HALF, 0:n], qT[pb:pb + DH, h // 2, q * P:(q + 1) * P],
                                       kT[pb:pb + DH, h // 2, k0:k0 + n], start=True, stop=True)
                    mm.then_inc(s_s, 1)

                def transposes(i):
                    q = steps[i][1]
                    pe.wait_ge(s_ex, i + 1)
                    if i >= 1:
                        pe.wait_ge(s_pta, taken(i - 1, True))
                        pe.wait_ge(s_ptd, taken(i - 1, False))
                    for k in range(q + 1):
                        mm = pe.transpose(PS[:, 4 + k // 4, (k % 4) * P:(k % 4 + 1) * P], Pm[:, i % 2, k * P:(k + 1) * P], ident[:])
                    mm.then_inc(s_pT, 1)

                def values(i):
                    h, q = steps[i]
                    pe.wait_ge(s_pta, taken(i, True))
                    pe.wait_ge(s_ptd, taken(i, False))
                    if i >= 2:
                        pe.wait_ge(s_oe, i - 1)
                    if i % 2:
                        pe.wait_ge(s_nb, key_terms[0])
                    for k in range(q + 1):
                        mm = pe.matmul(PS[:, 7 - i % 2, 0:DH], PT[:, i % 2, k, :], vr[:, k, h * DH:(h + 1) * DH],
                                       start=(k == 0), stop=(k == q))
                    mm.then_inc(s_pv, 1)

                pe.wait_ge(s_c2, 2)
                pe.wait_ge(s_cum, 1)
                key_term(0)
                key_term(1)
                score(0)
                score(1)
                for i, (h, q) in enumerate(steps):
                    transposes(i)
                    if i + 2 < NS:
                        score(i + 2)
                    if h + 1 < N_HEADS and q in (3, 5):
                        pe.wait_ge(s_oe, i - 1)
                        key_term(2 * (h + 1) + (q - 3) // 2)
                    if i:
                        values(i - 1)
                values(NS - 1)
                pe.wait_ge(s_wp, 16)
                pe.wait_ge(s_po, 1)
                pe.wait_ge(s_t2, NS)
                for t in range(NT):
                    if t >= 2:
                        pe.wait_ge(s_ye, t - 1)
                    for g in range(NG):
                        mm = pe.matmul(PS[:, t % 2, g * P:(g + 1) * P], uT[:, g, t * P:(t + 1) * P], wpl[:, g, :], start=True, stop=True)
                    mm.then_inc(s_yp, 1)

        woh = at("wo_hi", AT, [P, DC, D], F32R)
        wol = at("wo_lo", AT + 32, [P, DC, D], F32R)
        xt = at("xt", AT + 96, [P, 2, D], F32)
        x1 = at("x1", AT + 104, [P, 2, D], F32)
        h2 = at("h2", AT + 112, [P, 2, D], F32)
        mx = at("mx", AT + 120, [P, 2, D], F32)
        rows3 = at("rows3", AT + 128, [P, 4, D], F32)
        diag3 = at("diag3", AT + 144, [P, 2, DC, P], F32)
        mTh = at("mT_hi", AT + 152, [P, 2, DC, P], F32R)
        mTl = at("mT_lo", AT + 160, [P, 2, DC, P], F32R)
        gTh = at("gT_hi", AT + 168, [P, 2, DC, P], F32R)
        gTl = at("gT_lo", AT + 176, [P, 2, DC, P], F32R)
        wrr = at("wr_raw", AT + 184, [P, DC, N_EXPERTS], F32)
        wrh = at("wr_hi", AT + 186, [P, DC, N_EXPERTS], F32R)
        wrl = at("wr_lo", AT + 188, [P, DC, N_EXPERTS], F32R)
        score_t = at("score_t", AT + 190, [P, NT, N_EXPERTS], F32)
        junk = at("junk", AT + 192, [P, D], F32)
        GM, SF, BF, GX = range(4)

        s_wr = sem("s_wr")
        s_dg3 = sem("s_dg3")
        s_b3 = sem("s_b3")
        s_r3 = sem("s_r3")
        s_q3 = sem("s_q3")
        s_m3 = sem("s_m3")
        s_woh = sem("s_woh")
        s_wol = sem("s_wol")
        s_wrh = sem("s_wrh")
        s_wrl = sem("s_wrl")
        s_mx = sem("s_mx")
        s_tm = sem("s_tm")
        s_tmh = sem("s_tmh")
        s_tml = sem("s_tml")
        s_wp3 = sem("s_wp3")
        s_sq1 = sem("s_sq1")
        s_rt1 = sem("s_rt1")
        s_rs1 = sem("s_rs1")
        s_xa = sem("s_xa")
        s_x1 = sem("s_x1")
        s_sq2 = sem("s_sq2")
        s_rt2 = sem("s_rt2")
        s_rs2 = sem("s_rs2")
        s_ha = sem("s_ha")
        s_h2 = sem("s_h2")
        s_th = sem("s_th")
        s_thh = sem("s_thh")
        s_thl = sem("s_thl")
        s_lg = sem("s_lg")
        s_xl = [sem("s_xl0"), sem("s_xl1")]
        s_sx = [sem("s_sx0"), sem("s_sx1")]
        s_sh = [sem("s_sh0"), sem("s_sh1")]
        s_sig = sem("s_sig")

        def flat2(b):
            return PS[:, b:b + 2, :].rearrange("p a b -> p (a b)")

        def quads(b):
            return PS[:, b, :].rearrange("p (c m) -> p c m", c=4)

        with nc.Block() as block:
            @block.sync
            def _(sp):
                sp.dma_start(wrr[:], w_router[0].rearrange("(c p) n -> p c n", p=P)).then_inc(s_wr, 16)
                sp.wait_ge(s_woh, DC)
                sp.wait_ge(s_wol, DC)
                for t in range(2):
                    sp.dma_start(xt[:, t, :], x[0, t * P:(t + 1) * P, :]).then_inc(s_xl[t], 16)
                for t in range(NT):
                    b = t % 2
                    sp.wait_ge(s_x1, t + 1)
                    sp.dma_start(x1_dram[t * P:(t + 1) * P, :], x1[:, b, :]).then_inc(s_sx[b], 16)
                    if t + 2 < NT:
                        sp.dma_start(xt[:, b, :], x[0, (t + 2) * P:(t + 3) * P, :]).then_inc(s_xl[b], 16)
                    sp.wait_ge(s_h2, t + 1)
                    sp.dma_start(h2_dram[t * P:(t + 1) * P, :], h2[:, b, :]).then_inc(s_sh[b], 16)
                for b in range(2):
                    sp.wait_ge(s_sx[b], 16 * NT // 2)
                    sp.wait_ge(s_sh[b], 16 * NT // 2)

            @block.gpsimd
            def _(po):
                for t in range(NT):
                    b = t % 2
                    po.wait_ge(s_xa, t + 1)
                    po.wait_ge(s_xl[b], 16 * (t // 2 + 1))
                    po.tensor_tensor(x1[:, b, :], x1[:, b, :], xt[:, b, :], ALU.add).then_inc(s_x1, 1)
                    po.wait_ge(s_ha, t + 1)
                    po.tensor_tensor(h2[:, b, :], h2[:, b, :], rows3[:, BF, :], ALU.add).then_inc(s_h2, 1)

            @block.scalar
            def _(act):
                act.activation(root[:, 8:24], ssum[:, 0:16], ACT.Sqrt, bias=epsc[:, 0:1], scale=1.0 / HALF).then_inc(s_q3, 1)
                for dc in range(DC):
                    act.copy(woh[:, dc, :], woraw[:, dc, :]).then_inc(s_woh, 1)
                act.wait_ge(s_wr, 16)
                act.copy(wrh[:], wrr[:]).then_inc(s_wrh, 1)

                def mixed(t):
                    b = t % 2
                    for h in range(2):
                        act.wait_ge(s_tm, 2 * t + h + 1)
                        if t >= 2:
                            act.wait_ge(s_wp3, t - 1)
                        act.copy(mTh[:, b, 4 * h:4 * h + 4, :], quads(h)).then_inc(s_tmh, 1)

                def normed(t):
                    b = t % 2
                    for h in range(2):
                        act.wait_ge(s_th, 2 * t + h + 1)
                        if t >= 2:
                            act.wait_ge(s_lg, t - 1)
                        act.copy(gTh[:, b, 4 * h:4 * h + 4, :], quads(4 + h)).then_inc(s_thh, 1)

                mixed(0)
                for t in range(NT):
                    b = t % 2
                    if t + 1 < NT:
                        mixed(t + 1)
                    if t:
                        normed(t - 1)
                    act.wait_ge(s_wp3, t + 1)
                    act.activation(junk[:], flat2(2), ACT.Square, accum_out=ssum[:, 16 + t:17 + t]).then_inc(s_sq1, 1)
                    act.wait_ge(s_sq1, 2 * t + 1)
                    act.activation(root[:, 24 + t:25 + t], ssum[:, 16 + t:17 + t], ACT.Sqrt, bias=epsc[:, 0:1], scale=1.0 / D).then_inc(s_rt1, 1)
                    act.wait_ge(s_x1, t + 1)
                    act.activation(junk[:], x1[:, b, :], ACT.Square, accum_out=ssum[:, 24 + t:25 + t]).then_inc(s_sq1, 1)
                    act.wait_ge(s_sq1, 2 * t + 2)
                    act.activation(root[:, 32 + t:33 + t], ssum[:, 24 + t:25 + t], ACT.Sqrt, bias=epsc[:, 0:1], scale=1.0 / D).then_inc(s_rt2, 1)
                normed(NT - 1)
                act.wait_ge(s_lg, NT)
                act.activation(score_t[:], PS[:, 6, :].rearrange("p (t e) -> p t e", t=NT), ACT.Sigmoid).then_inc(s_sig, 1)

            @block.vector
            def _(v):
                v.wait_ge(s_q3, 1)
                v.reciprocal(rstd[:, 8:24], root[:, 8:24]).then_inc(s_m3, 1)
                cols = (vecc[:, 1, :], vecc[:, 2, :], modc[:, 24:32], pcol[:, C_GMIX:C_GMIX + 8])
                for i, col in enumerate(cols):
                    if i >= 2:
                        v.wait_ge(s_b3, i - 1)
                    v.tensor_tensor(diag3[:, i % 2], ident[:, None, :].broadcast_to([P, DC, P]),
                                    col[:, :, None].broadcast_to([P, DC, P]), ALU.mult).then_inc(s_dg3, 1)
                    if i:
                        v.wait_ge(s_b3, i)
                        v.tensor_copy(rows3[:, i - 1, :], flat2(((i - 1) % 2) * 2)).then_inc(s_r3, 1)
                v.wait_ge(s_b3, 4)
                v.tensor_copy(rows3[:, 3, :], flat2(2)).then_inc(s_r3, 1)
                v.wait_ge(s_r3, 4)
                for dc in range(DC):
                    v.wait_ge(s_woh, dc + 1)
                    v.tensor_tensor(wol[:, dc, :], woraw[:, dc, :], woh[:, dc, :].bitcast(F32), ALU.subtract).then_inc(s_wol, 1)
                v.wait_ge(s_wrh, 1)
                v.tensor_tensor(wrl[:], wrr[:], wrh[:].bitcast(F32), ALU.subtract).then_inc(s_wrl, 1)
                v.wait_ge(s_m3, 1)
                v.wait_ge(s_wol, DC)

                def scale_mixed(t):
                    b = t % 2
                    if t >= 2:
                        v.wait_ge(s_tm, 2 * (t - 1))
                    v.scalar_tensor_tensor(mx[:, b, 0:HALF], ymix[:, t, 0:HALF], rstd[:, 8 + t:9 + t], rows3[:, GX, 0:HALF],
                                           ALU.mult, ALU.mult).then_inc(s_mx, 1)
                    v.scalar_tensor_tensor(mx[:, b, HALF:D], ymix[:, t, HALF:D], rstd[:, 16 + t:17 + t], rows3[:, GX, HALF:D],
                                           ALU.mult, ALU.mult).then_inc(s_mx, 1)

                def mixed(t):
                    b = t % 2
                    for h in range(2):
                        v.wait_ge(s_tmh, 2 * t + h + 1)
                        v.tensor_tensor(mTl[:, b, 4 * h:4 * h + 4, :], quads(h), mTh[:, b, 4 * h:4 * h + 4, :].bitcast(F32),
                                        ALU.subtract).then_inc(s_tml, 1)

                def normed(t):
                    b = t % 2
                    for h in range(2):
                        v.wait_ge(s_thh, 2 * t + h + 1)
                        v.tensor_tensor(gTl[:, b, 4 * h:4 * h + 4, :], quads(4 + h), gTh[:, b, 4 * h:4 * h + 4, :].bitcast(F32),
                                        ALU.subtract).then_inc(s_thl, 1)

                scale_mixed(0)
                scale_mixed(1)
                mixed(0)
                for t in range(NT):
                    b = t % 2
                    if t + 1 < NT:
                        mixed(t + 1)
                    if t + 2 < NT:
                        scale_mixed(t + 2)
                    if t:
                        normed(t - 1)
                    v.wait_ge(s_rt1, t + 1)
                    v.reciprocal(rstd[:, 24 + t:25 + t], root[:, 24 + t:25 + t]).then_inc(s_rs1, 1)
                    v.wait_ge(s_rs1, t + 1)
                    if t >= 2:
                        v.wait_ge(s_sx[b], 16 * (t // 2))
                    v.scalar_tensor_tensor(x1[:, b, :], flat2(2), rstd[:, 24 + t:25 + t], rows3[:, GM, :],
                                           ALU.mult, ALU.mult).then_inc(s_xa, 1)
                    v.wait_ge(s_rt2, t + 1)
                    v.reciprocal(rstd[:, 32 + t:33 + t], root[:, 32 + t:33 + t]).then_inc(s_rs2, 1)
                    v.wait_ge(s_rs2, t + 1)
                    if t >= 2:
                        v.wait_ge(s_sh[b], 16 * (t // 2))
                    v.scalar_tensor_tensor(h2[:, b, :], x1[:, b, :], rstd[:, 32 + t:33 + t], rows3[:, SF, :],
                                           ALU.mult, ALU.mult).then_inc(s_ha, 1)
                normed(NT - 1)

            @block.tensor
            def _(pe):
                for i in range(4):
                    pe.wait_ge(s_dg3, i + 1)
                    if i >= 2:
                        pe.wait_ge(s_r3, i - 1)
                    for h in range(2):
                        mm = pe.matmul(PS[:, (i % 2) * 2 + h, :], ones[:], diag3[:, i % 2, 4 * h:4 * h + 4, :], start=True, stop=True)
                    mm.then_inc(s_b3, 1)
                pe.wait_ge(s_r3, 4)

                def mixed(t):
                    pe.wait_ge(s_mx, 2 * t + 2)
                    for h in range(2):
                        if t:
                            pe.wait_ge(s_tml, 2 * (t - 1) + h + 1)
                        for q in range(4):
                            mm = pe.transpose(PS[:, h, q * P:(q + 1) * P], mx[:, t % 2, (4 * h + q) * P:(4 * h + q + 1) * P], ident[:])
                        mm.then_inc(s_tm, 1)

                def normed(t):
                    b = t % 2
                    pe.wait_ge(s_h2, t + 1)
                    for h in range(2):
                        if t:
                            pe.wait_ge(s_thl, 2 * (t - 1) + h + 1)
                        for q in range(4):
                            mm = pe.transpose(PS[:, 4 + h, q * P:(q + 1) * P], h2[:, b, (4 * h + q) * P:(4 * h + q + 1) * P], ident[:])
                        mm.then_inc(s_th, 1)
                    pe.wait_ge(s_thh, 2 * t + 2)
                    pe.wait_ge(s_thl, 2 * t + 2)
                    n = 0
                    for dc in range(DC):
                        for ht, wt in ((gTh, wrh), (gTh, wrl), (gTl, wrh)):
                            mm = pe.matmul(PS[:, 6, t * N_EXPERTS:(t + 1) * N_EXPERTS], ht[:, b, dc, :], wt[:, dc, :],
                                           start=(n == 0), stop=(n == 3 * DC - 1))
                            n += 1
                    mm.then_inc(s_lg, 1)

                mixed(0)
                for t in range(NT):
                    b = t % 2
                    if t + 1 < NT:
                        mixed(t + 1)
                    pe.wait_ge(s_tmh, 2 * t + 2)
                    pe.wait_ge(s_tml, 2 * t + 2)
                    pe.wait_ge(s_wol, DC)
                    if t:
                        pe.wait_ge(s_xa, t)
                    for h in range(2):
                        n = 0
                        for dc in range(DC):
                            for mt, wt in ((mTh, woh), (mTh, wol), (mTl, woh)):
                                mm = pe.matmul(PS[:, 2 + h, :], mt[:, b, dc, :], wt[:, dc, h * HALF:(h + 1) * HALF],
                                               start=(n == 0), stop=(n == 3 * DC - 1))
                                n += 1
                    mm.then_inc(s_wp3, 1)
                    if t:
                        if t == 1:
                            pe.wait_ge(s_wrl, 1)
                        normed(t - 1)
                normed(NT - 1)

        biasr = at("bias_row", AT, [P, N_EXPERTS], F32)
        sel = at("sel", AT + 0.25, [P, NT, N_EXPERTS], F32)
        top2 = at("top2", AT + 2.25, [P, NT * N_GROUPS, 8], F32)
        gsum = at("gsum", AT + 4.25, [P, NT, N_GROUPS], F32)
        cmp1 = at("cmp1", AT + 4.5, [P, NT, N_GROUPS, N_GROUPS], F32)
        cmp2 = at("cmp2", AT + 6.5, [P, NT, N_GROUPS, N_GROUPS], F32)
        before = at("before", AT + 8.5, [P, N_GROUPS, N_GROUPS], F32)
        grank = at("grank", AT + 8.75, [P, NT * N_GROUPS], F32)
        gpen = at("gpen", AT + 9, [P, NT * N_GROUPS], F32)
        selm = at("selm", AT + 9.25, [P, NT, N_EXPERTS], F32)
        top8 = at("top8", AT + 11.25, [P, NT, 8], F32)
        repl = at("repl", AT + 11.5, [P, NT, N_EXPERTS], F32)
        mask = at("mask", AT + 13.5, [P, NT, N_EXPERTS], F32)
        maskb = at("maskb", AT + 15.5, [P, NT, N_EXPERTS], BF16)
        wts = at("wts", AT + 16.5, [P, NT, N_EXPERTS], F32)
        wsum = at("wsum", AT + 18.5, [P, 4, NT], F32)
        utri = at("utri", AT + 19, [P, P], BF16)
        onesb = at("onesb", AT + 19.25, [P, P], BF16)
        utrif = at("utrif", AT + 19.5, [P, P], F32)
        erow = at("erow", AT + 20, [P, 12, N_EXPERTS], F32)
        erowi = at("erowi", AT + 23, [P, 2, N_EXPERTS], I32)
        pos = at("pos", AT + 23.5, [P, NT, N_EXPERTS], F32)
        pos8 = at("pos8", AT + 25.5, [P, NT, 8], F32)
        posi = at("posi", AT + 25.75, [P, 3, NT * 8], I32)
        blk8 = at("blk8", AT + 26.5, [P, NT * 8], F32)
        slt8 = at("slt8", AT + 26.75, [P, NT * 8], F32)
        w8 = at("w8", AT + 27, [P, NT * 8], F32)
        ojunk = at("ojunk", AT + 64, [P, NT * TOP_K + 1, N_EXPERTS], F32)
        ioti = at("iota_i", AT + 27.5, [P, P], I32)
        iotf = at("iota_f", AT + 28, [P, P], F32)
        tokf = at("tok1_f", AT + 28.5, [P, 16], F32)
        toki = at("tok1_i", AT + 28.5625, [P, 16], I32)
        NB4 = 4
        onea = at("onehot_slot", AT + 29, [P, NB4, P], F32)
        oneb = at("onehot_block", AT + 31, [P, NB4, 2, P], F32)
        tabf = at("tab_f", AT + 35, [P, 4, P], F32)
        rcol = at("rcol", AT + 37, [P, 8], F32)
        rowf = at("rowf", AT + 38, [P, 3, TAB], F32)
        zero_t = at("zero_t", AT + 40, [P, D], F32)

        s_ri = sem("s_ri")
        s_rk = sem("s_rk")
        s_bl = sem("s_bl")
        s_mb = sem("s_mb")
        s_cm = sem("s_cm")
        s_oa = sem("s_oa")
        s_ob = sem("s_ob")
        s_tb = sem("s_tb")
        s_s8 = sem("s_s8")
        s_rc2 = sem("s_rc2")
        s_rt4 = sem("s_rt4")
        s_zt = sem("s_zt")
        s_zd = sem("s_zd")
        PAIRS = [(t, k) for t in range(NT) for k in range(TOP_K)]
        (NBK, PEND, PSTA, ACTV, CACT, PBASE, ONE, CNT) = range(8)

        with nc.Block() as block:
            @block.sync
            def _(sp):
                sp.dma_start(biasr[:], router_bias.broadcast_to([P, N_EXPERTS])).then_inc(s_bl, 16)
                sp.wait_ge(s_zt, 1)
                sp.dma_start(acc_dram[T:T + P, :], zero_t[:]).then_inc(s_zd, 16)
                sp.wait_ge(s_zd, 16)

            @block.gpsimd
            def _(po):
                po.memset(utrif[:], 1.0).then_inc(s_ri, 1)
                po.memset(before[:], 1.0).then_inc(s_ri, 1)
                po.memset(onesb[:], 1.0).then_inc(s_ri, 1)
                po.iota(ioti[:], [[1, P]], base=0, channel_multiplier=0).then_inc(s_ri, 1)
                po.iota(toki[:, 0:NT], [[P, NT]], base=1, channel_multiplier=1).then_inc(s_ri, 1)
                po.wait_ge(s_ri, 5)
                po.affine_select(out=utrif[:], in_=utrif[:], compare_op=ALU.is_gt, fill=0.0, base=0,
                                 pattern=[[1, P]], channel_multiplier=-1).then_inc(s_ri, 1)
                po.affine_select(out=before[:], in_=before[:], compare_op=ALU.is_gt, fill=0.0, base=0,
                                 pattern=[[1, N_GROUPS], [-1, N_GROUPS]], channel_multiplier=0).then_inc(s_ri, 1)
                po.tensor_copy(iotf[:], ioti[:]).then_inc(s_ri, 1)
                po.tensor_copy(tokf[:, 0:NT], toki[:, 0:NT]).then_inc(s_ri, 1)
                po.wait_ge(s_ri, 9)
                po.tensor_copy(utri[:], utrif[:]).then_inc(s_ri, 1)
                po.memset(zero_t[:], 0.0).then_inc(s_zt, 1)
                po.memset(gidx[:], SKIP).then_inc(s_ri, 1)
                po.memset(sidx[:], 0).then_inc(s_ri, 1)
                po.memset(wtab[:], 0.0).then_inc(s_ri, 1)
                po.memset(btab[0:1], 0).then_inc(s_ri, 1)
                po.memset(erow[:, ONE, :], 1.0).then_inc(s_ri, 1)
                po.memset(rowf[0:1], 0.0).then_inc(s_ri, 1)
                po.wait_ge(s_s8, 1)
                for n in range(len(PAIRS)):
                    if n >= NB4:
                        po.wait_ge(s_tb, n - NB4 + 1)
                    po.tensor_scalar(onea[:, n % NB4, :], iotf[:], slt8[:, n:n + 1], None, ALU.is_equal).then_inc(s_oa, 1)

            @block.vector
            def _(v):
                n = [0]

                def link(ins):
                    n[0] += 1
                    ins.then_inc(s_rk, 1)
                    v.wait_ge(s_rk, n[0])

                def step(ins):
                    n[0] += 1
                    ins.then_inc(s_rk, 1)

                v.wait_ge(s_bl, 16)
                v.wait_ge(s_ri, 16)
                link(v.tensor_tensor(sel[:], score_t[:], biasr[:, None, :].broadcast_to([P, NT, N_EXPERTS]), ALU.add))
                for t in range(NT):
                    for g in range(N_GROUPS):
                        step(v.max(out=top2[:, t * N_GROUPS + g, :], in_=sel[:, t, g * PER_GROUP:(g + 1) * PER_GROUP]))
                v.wait_ge(s_rk, n[0])
                gs = gsum[:].rearrange("p t g -> p (t g)")
                link(v.tensor_tensor(gs, top2[:, :, 0], top2[:, :, 1], ALU.add))
                mine = gsum[:, :, :, None].broadcast_to([P, NT, N_GROUPS, N_GROUPS])
                other = gsum[:, :, None, :].broadcast_to([P, NT, N_GROUPS, N_GROUPS])
                step(v.tensor_tensor(cmp1[:], other, mine, ALU.is_gt))
                link(v.tensor_tensor(cmp2[:], other, mine, ALU.is_equal))
                c2 = cmp2[:].rearrange("p t g j -> p t (g j)")
                bf = before[:].rearrange("p g j -> p (g j)")
                link(v.tensor_tensor(c2, c2, bf[:, None, :].broadcast_to([P, NT, 64]), ALU.mult))
                link(v.tensor_tensor(cmp1[:], cmp1[:], cmp2[:], ALU.add))
                link(v.tensor_reduce(grank[:], cmp1[:].rearrange("p t g j -> p (t g) j"), AX, ALU.add))
                link(v.tensor_scalar(gpen[:], grank[:], float(TOP_GROUPS), BIG, ALU.is_lt, ALU.mult))
                link(v.tensor_scalar(gpen[:], gpen[:], BIG, None, ALU.subtract))
                link(v.tensor_tensor(selm[:].rearrange("p t (g e) -> p (t g) e", g=N_GROUPS),
                                     sel[:].rearrange("p t (g e) -> p (t g) e", g=N_GROUPS),
                                     gpen[:, :, None].broadcast_to([P, NT * N_GROUPS, PER_GROUP]), ALU.add))
                for t in range(NT):
                    step(v.max(out=top8[:, t, :], in_=selm[:, t, :]))
                v.wait_ge(s_rk, n[0])
                for t in range(NT):
                    step(v.match_replace(out=repl[:, t, :], in_to_replace=top8[:, t, :], in_values=selm[:, t, :], imm_value=LOWEST))
                v.wait_ge(s_rk, n[0])
                link(v.tensor_tensor(mask[:], repl[:], selm[:], ALU.not_equal))
                v.tensor_copy(maskb[:], mask[:]).then_inc(s_mb, 1)
                link(v.tensor_tensor(wts[:], score_t[:], mask[:], ALU.mult))
                link(v.tensor_reduce(wsum[:, 0, :], wts[:], AX, ALU.add))
                link(v.reciprocal(wsum[:, 1, :], wsum[:, 0, :]))
                link(v.tensor_scalar(wsum[:, 2, :], wsum[:, 1, :], ROUTED_SCALE, None, ALU.mult))
                link(v.tensor_tensor(wts[:], wts[:], wsum[:, 2, :][:, :, None].broadcast_to([P, NT, N_EXPERTS]), ALU.mult))
                v.wait_ge(s_cm, 1)
                link(v.tensor_scalar(erowi[:, 0, :], PS[:, 1, 0:N_EXPERTS], float(P - 1), None, ALU.add))
                link(v.tensor_scalar(erowi[:, 1, :], erowi[:, 0, :], 7, None, ALU.arith_shift_right))
                link(v.tensor_copy(erow[:, NBK, :], erowi[:, 1, :]))
                link(v.tensor_tensor_scan(erow[:, PEND, :], erow[:, ONE, :], erow[:, NBK, :], 0.0, ALU.mult, ALU.add))
                link(v.tensor_tensor(erow[:, PSTA, :], erow[:, PEND, :], erow[:, NBK, :], ALU.subtract))
                link(v.tensor_scalar(erow[:, ACTV, :], erow[:, NBK, :], 0.0, None, ALU.is_gt))
                link(v.tensor_tensor_scan(erow[:, CACT, :], erow[:, ONE, :], erow[:, ACTV, :], 0.0, ALU.mult, ALU.add))
                link(v.tensor_scalar(erow[:, PBASE, :], erow[:, PSTA, :], float(P), 1.0, ALU.mult, ALU.add))
                link(v.tensor_tensor(pos[:], PS[:, 0, :].rearrange("p (t e) -> p t e", t=NT),
                                     erow[:, PBASE, :][:, None, :].broadcast_to([P, NT, N_EXPERTS]), ALU.add))
                link(v.tensor_tensor(pos[:], pos[:], mask[:], ALU.mult))
                link(v.tensor_scalar(pos[:], pos[:], -1.0, None, ALU.add))
                for t in range(NT):
                    step(v.max(out=pos8[:, t, :], in_=pos[:, t, :]))
                v.wait_ge(s_rk, n[0])
                link(v.tensor_copy(posi[:, 0, :], pos8[:].rearrange("p t k -> p (t k)")))
                step(v.tensor_scalar(posi[:, 1, :], posi[:, 0, :], 7, None, ALU.arith_shift_right))
                link(v.tensor_scalar(posi[:, 2, :], posi[:, 0, :], P - 1, None, ALU.bitwise_and))
                step(v.tensor_copy(blk8[:], posi[:, 1, :]))
                v.tensor_copy(slt8[:], posi[:, 2, :]).then_inc(s_s8, 1)
                for i, (t, k) in enumerate(PAIRS):
                    step(v.scalar_tensor_tensor(ojunk[:, i, :], pos[:, t, :], pos8[:, t, k:k + 1], wts[:, t, :],
                                                ALU.is_equal, ALU.mult, accum_out=w8[:, i:i + 1]))
                v.wait_ge(s_rk, n[0])
                for i, (t, k) in enumerate(PAIRS):
                    if i >= NB4:
                        v.wait_ge(s_tb, i - NB4 + 1)
                    v.tensor_scalar(oneb[:, i % NB4, 0, :], iotf[:], blk8[:, i:i + 1], tokf[:, t:t + 1], ALU.is_equal, ALU.mult).then_inc(s_ob, 1)
                    v.tensor_scalar(oneb[:, i % NB4, 1, :], iotf[:], blk8[:, i:i + 1], w8[:, i:i + 1], ALU.is_equal, ALU.mult).then_inc(s_ob, 1)
                v.wait_ge(s_tb, len(PAIRS))
                tok = PS[:, 2, 0:P]
                step(v.tensor_copy(wtab[:, 0:P], PS[:, 2, P:2 * P]))
                step(v.tensor_scalar(tabf[:, 0, :], tok, 0.0, None, ALU.is_equal))
                step(v.tensor_scalar(tabf[:, 1, :], tok, -1.0, None, ALU.add))
                link(v.tensor_scalar(rcol[:, 0:1], tokf[:, 0:1], float(T), None, ALU.add))
                step(v.scalar_tensor_tensor(gidx[:, 0:P], tabf[:, 0, :], float(SKIP), tabf[:, 1, :], ALU.mult, ALU.add))
                step(v.scalar_tensor_tensor(sidx[:, 0:P], tabf[:, 0, :], rcol[:, 0:1], tabf[:, 1, :], ALU.mult, ALU.add))
                link(v.tensor_scalar(rcol[:, 1:2], tokf[:, 0:1], -1.0, None, ALU.add))
                step(v.scalar_tensor_tensor(ojunk[:, NT * TOP_K, :], erow[:, PSTA, :], rcol[:, 1:2], erow[:, ACTV, :],
                                            ALU.is_le, ALU.mult, accum_out=rcol[:, 2:3]))
                step(v.scalar_tensor_tensor(tabf[:, 2, 0:N_EXPERTS], erow[:, CACT, :], rcol[:, 1:2], erow[:, ONE, :],
                                            ALU.is_le, ALU.mult, accum_out=rcol[:, 3:4]))
                v.wait_ge(s_rk, n[0])
                v.engine_nop().then_inc(s_rc2, 1)
                v.wait_ge(s_rt4, 1)
                step(v.tensor_copy(rowf[0:1, 0, 1:P + 1], PS[0:1, 3, 0:P]))
                link(v.tensor_scalar(rowf[0:1, 1, 0:P], PS[0:1, 3, P:2 * P], float(N_EXPERTS - 1), None, ALU.min))
                step(v.tensor_copy(btab[0:1, 0, 0:P], rowf[0:1, 0, 1:P + 1]))
                step(v.tensor_tensor(btab[0:1, 1, 0:P], rowf[0:1, 0, 1:P + 1], rowf[0:1, 0, 0:P], ALU.subtract))
                link(v.tensor_copy(etab[0:1, 0:P], rowf[0:1, 1, 0:P]))
                step(v.tensor_scalar(btab[0:1, 2, 0:P], btab[0:1, 0, 0:P], 1, None, ALU.bitwise_and))
                step(v.tensor_scalar(btab[0:1, 4, 0:P], btab[0:1, 0, 0:P], 1, None, ALU.arith_shift_right))
                step(v.tensor_scalar(btab[0:1, 5, 0:1], erow[0:1, CACT, N_EXPERTS - 1:N_EXPERTS], 1.0, None, ALU.add))
                link(v.tensor_scalar(btab[0:1, 5, 1:2], erow[0:1, PEND, N_EXPERTS - 1:N_EXPERTS], 1.0, None, ALU.add))
                step(v.tensor_tensor(btab[0:1, 3, 0:P], btab[0:1, 4, 0:P], btab[0:1, 2, 0:P], ALU.add))
                link(v.tensor_scalar(btab[0:1, 5, 2:4], btab[0:1, 5, 0:2], 1, 1, ALU.arith_shift_right, ALU.arith_shift_left))

            @block.tensor
            def _(pe):
                pe.wait_ge(s_ri, 10)
                pe.wait_ge(s_mb, 1)
                for t in range(NT):
                    for u in range(t + 1):
                        mm = pe.matmul(PS[:, 0, t * N_EXPERTS:(t + 1) * N_EXPERTS], (utri if u == t else onesb)[:], maskb[:, u, :],
                                       start=(u == 0), stop=(u == t))
                for u in range(NT):
                    mm = pe.matmul(PS[:, 1, 0:N_EXPERTS], onesb[:], maskb[:, u, :], start=(u == 0), stop=(u == NT - 1))
                mm.then_inc(s_cm, 1)
                for i in range(len(PAIRS)):
                    pe.wait_ge(s_oa, i + 1)
                    pe.wait_ge(s_ob, 2 * i + 2)
                    pe.matmul(PS[:, 2, 0:2 * P], onea[:, i % NB4, :], oneb[:, i % NB4].rearrange("p a b -> p (a b)"),
                              start=(i == 0), stop=(i == len(PAIRS) - 1)).then_inc(s_tb, 1)
                pe.wait_ge(s_rc2, 1)
                pe.matmul(PS[0:1, 3, 0:P], rcol[:, 2:3], ident[:], start=True, stop=True)
                pe.matmul(PS[0:1, 3, P:2 * P], rcol[:, 3:4], ident[:], start=True, stop=True).then_inc(s_rt4, 1)

        eraw = at("eraw", AT, [P, 2, 3, UNIT], F32)
        eh = at("e_hi", AT + 48, [P, 2, 3, UNIT], F32R)
        el = at("e_lo", AT + 96, [P, 2, 3, UNIT], F32R)
        xg = [at("xgA", AT + 144, [P, D], F32), at("xgB", AT + 148, [P, D], F32)]
        xh = [at("xhA", AT + 152, [P, DC, P], F32R), at("xhB", AT + 156, [P, DC, P], F32R)]
        xl = [at("xlA", AT + 160, [P, DC, P], F32R), at("xlB", AT + 164, [P, DC, P], F32R)]
        yb = [at("ybA", AT + 168, [P, D], F32), at("ybB", AT + 172, [P, D], F32)]
        sg = [at("sgA", AT + 176, [P, F], F32), at("sgB", AT + 177, [P, F], F32)]
        ga = [at("gaA", AT + 178, [P, F], F32), at("gaB", AT + 179, [P, F], F32)]
        ah = [at("ahA", AT + 180, [P, FC, P], F32R), at("ahB", AT + 181, [P, FC, P], F32R)]
        al = [at("alA", AT + 182, [P, FC, P], F32R), at("alB", AT + 183, [P, FC, P], F32R)]
        GU0, XT0, AT0, Y0 = 0, 2, (4, 7), 5
        GU_PARTS, DN_PARTS = 4, 2
        GU_W, DN_W = UNIT // GU_PARTS, UNIT // DN_PARTS

        e_gu = [sem("e_gate_up_even"), sem("e_gate_up_odd")]
        e_dn = [sem("e_down_even"), sem("e_down_odd")]
        e_rg = sem("e_gate_up_landed")
        e_rd = sem("e_down_landed")
        e_hgu = sem("e_gate_up_hi")
        e_lgu = sem("e_gate_up_lo")
        e_hd = sem("e_down_hi")
        e_ld = sem("e_down_lo")
        e_g = [sem("e_gathered_a"), sem("e_gathered_b")]
        e_x = sem("e_x_transposed")
        e_xh = sem("e_x_hi")
        e_xl = sem("e_x_lo")
        e_p = sem("e_gate_up_done")
        e_s = sem("e_sigmoid")
        e_w = sem("e_weighted")
        e_a = sem("e_act")
        e_t = sem("e_act_transposed")
        e_ah = sem("e_act_hi")
        e_al = sem("e_act_lo")
        e_y = sem("e_down_done")
        e_ye = sem("e_y_copied")
        e_o = [sem("e_added_a"), sem("e_added_b")]
        e_ig = sem("e_gather_indices")
        e_is = sem("e_scatter_indices")
        SHB = NT

        wg_v = w_gate[0].rearrange("e (p c) n -> e p (c n)", p=P)
        wu_v = w_up[0].rearrange("e (p c) n -> e p (c n)", p=P)
        wd_v = w_down[0].rearrange("e (p c) n -> e p (c n)", p=P)

        def entry(eng, row, b, hi):
            return eng.value_load(btab[0:1, row, bass.ds(b, 1)], min_val=0, max_val=hi)

        def n_blocks(eng):
            return eng.value_load(btab[0:1, 5, 3:4], min_val=2, max_val=P)

        with nc.Block() as block:
            @block.sync
            def _(sp):
                sp.dma_start(eraw[:, 0, 0, :], ws_gate[0].rearrange("(p c) n -> p (c n)", p=P)).then_inc(e_gu[0], 16)
                sp.dma_start(eraw[:, 0, 1, :], ws_up[0].rearrange("(p c) n -> p (c n)", p=P)).then_inc(e_gu[0], 16)
                sp.dma_start(eraw[:, 0, 2, :], ws_down[0].rearrange("(p c) n -> p (c n)", p=P)).then_inc(e_dn[0], 16)

                def expert(at_rank):
                    return sp.value_load(etab[0:1, at_rank], min_val=0, max_val=N_EXPERTS - 1)

                def load_gate_up(slot, e):
                    for k, w in enumerate((wg_v, wu_v)):
                        sp.dma_start(eraw[:, slot, k, :], w[bass.ds(e, 1)].rearrange("e p n -> p (e n)")).then_inc(e_gu[slot], 16)

                def load_down(slot, e):
                    sp.dma_start(eraw[:, slot, 2, :], wd_v[bass.ds(e, 1)].rearrange("e p n -> p (e n)")).then_inc(e_dn[slot], 16)

                used = sp.value_load(btab[0:1, 5, 2:3], min_val=TOP_K, max_val=N_EXPERTS)
                first, second = expert(slice(0, 1)), expert(slice(1, 2))
                load_gate_up(1, first)
                load_down(1, first)
                sp.wait_ge(e_lgu, GU_PARTS)
                load_gate_up(0, second)
                sp.wait_ge(e_gu[1], 32)
                sp.sem_inc(e_rg, 1)
                sp.wait_ge(e_ld, DN_PARTS)
                load_down(0, second)
                sp.wait_ge(e_dn[1], 16)
                sp.sem_inc(e_rd, 1)
                with sp.Fori(3, used + 1, 2) as r:
                    for j in range(2):
                        e = expert(bass.ds(r + j - 1, 1))
                        sp.wait_ge(e_lgu, (r + j - 1) * GU_PARTS)
                        load_gate_up(1 - j, e)
                        sp.wait_ge(e_gu[j], r * 16 + 16)
                        sp.sem_inc(e_rg, 1)
                        sp.wait_ge(e_ld, (r + j - 1) * DN_PARTS)
                        load_down(1 - j, e)
                        sp.wait_ge(e_dn[j], r * 8 + 8)
                        sp.sem_inc(e_rd, 1)
                sp.wait_ge(e_gu[0], used * 16 + 32)
                sp.sem_inc(e_rg, 1)
                sp.wait_ge(e_dn[0], used * 8 + 16)
                sp.sem_inc(e_rd, 1)

            @block.gpsimd
            def _(po):
                def fetch(j, X, b):
                    po.wait_ge(e_x, X * 2 - 2)
                    if b is None:
                        po.dma_start(xg[j][:], h2_dram[bass.ds(X * P, P), :]).then_inc(e_g[j], 16)
                        return
                    po.tensor_copy(gnow[:, j, 0:1], gidx[:, bass.ds(b, 1)]).then_inc(e_ig, 2)
                    po.wait_ge(s_sh[j], 16)
                    po.wait_ge(e_ig, X * 2 - 2)
                    po.indirect_dma_start(xg[j][:], None, h2_dram[:, :], bass.IndirectOffsetOnAxis(ap=gnow[:, j, 0:1], axis=0),
                                          bounds_check=T - 1, oob_is_err=False).then_inc(e_g[j], 16)

                def results(j, G, b):
                    if b is None:
                        po.wait_ge(e_ye, (G + j) * 2 + 2)
                        po.dma_start(acc_dram[bass.ds((G + j) * P, P), :], yb[j][:]).then_inc(e_o[j], 16)
                        return
                    po.wait_ge(e_o[1 - j], G * 8 + 16 * j)
                    po.wait_ge(e_ye, (G + j) * 2 + 2)
                    po.tensor_copy(snow[:, j, 0:1], sidx[:, bass.ds(b, 1)]).then_inc(e_is, 2)
                    po.wait_ge(s_zd, 16)
                    po.wait_ge(e_is, (G + j) * 2 + 2)
                    po.indirect_dma_start(acc_dram[:, :], bass.IndirectOffsetOnAxis(ap=snow[:, j, 0:1], axis=0), yb[j][:], None,
                                          compute_op=ALU.add).then_inc(e_o[j], 16)

                po.sem_inc(e_ig, 2 * SHB - 4)
                po.sem_inc(e_is, 2 * SHB)
                for j in range(2):
                    po.dma_start(xg[j][:], h2_dram[j * P:(j + 1) * P, :]).then_inc(e_g[j], 16)
                fetch(0, 2, None)
                with po.Fori(0, SHB - 5, 2) as G:
                    for j in range(2):
                        fetch(1 - j, G + j + 3, None)
                        results(j, G, None)
                for X in range(SHB - 4, SHB):
                    fetch(1 - X % 2, X + 3, None if X + 3 < SHB else X + 3 - SHB)
                    results(X % 2, X - X % 2, None)
                with po.Fori(0, n_blocks(po), 2) as b:
                    for j in range(2):
                        fetch(1 - j, b + (SHB + j + 3), b + (j + 3))
                        results(j, b + SHB, b + j)
                used = po.value_load(btab[0:1, 5, 2:3], min_val=TOP_K, max_val=N_EXPERTS)
                n = n_blocks(po)
                for i in range(2):
                    po.wait_ge(e_gu[i], used * 16 + 32 * (1 - i))
                    po.wait_ge(e_dn[i], used * 8 + 16 * (1 - i))
                for j in range(2):
                    po.wait_ge(e_g[j], n * 8 + 8 * SHB + 32 - 16 * j)
                    po.wait_ge(e_o[j], n * 8 + 8 * SHB)

            def split_engine(eng, high):

                def views(slot, k0, k1, c0, c1):
                    if isinstance(slot, int):
                        return tuple(w[:, slot, k0:k1, c0:c1] for w in (eh, eraw, el))
                    return tuple(w[:, bass.ds(slot, 1), k0:k1, c0:c1].rearrange("p s k n -> p (s k) n") for w in (eh, eraw, el))

                def part(rank, parts, i, view, hi_done, lo_done):
                    hi, src, lo = view
                    if high:
                        eng.copy(hi, src).then_inc(hi_done, 1)
                    else:
                        eng.wait_ge(hi_done, rank * parts + i + 1)
                        eng.tensor_tensor(lo, src, hi.bitcast(F32), ALU.subtract).then_inc(lo_done, 1)

                def gate_up(rank, slot):
                    for i in range(GU_PARTS):
                        part(rank, GU_PARTS, i, views(slot, 0, 2, i * GU_W, (i + 1) * GU_W), e_hgu, e_lgu)

                def down(rank, slot):
                    for i in range(DN_PARTS):
                        part(rank, DN_PARTS, i, views(slot, 2, 3, i * DN_W, (i + 1) * DN_W), e_hd, e_ld)

                def if_new(split, b, landed):
                    fresh = entry(eng, 1, b, 1)
                    with eng.If(fresh):
                        rank = entry(eng, 0, b, N_EXPERTS)
                        slot = entry(eng, 2, b, 1)
                        if high:
                            eng.wait_ge(landed, rank)
                        split(rank, slot)

                def new_gate_up(b):
                    if_new(gate_up, b, e_rg)

                def new_down(b):
                    if_new(down, b, e_rd)

                return gate_up, down, new_gate_up, new_down

            def quads_of(bank):
                return PS[:, bank, :].rearrange("p (c m) -> p c m", c=4)

            @block.scalar
            def _(act):
                gate_up, down, new_gate_up, new_down = split_engine(act, True)

                def sigmoid(j, X):
                    act.wait_ge(e_p, X + 1)
                    act.activation(sg[j][:], PS[:, GU0 + j, 0:F], ACT.Sigmoid).then_inc(e_s, 1)

                def x_high(j, X):
                    for h in range(2):
                        act.wait_ge(e_x, X * 2 + h + 1)
                        act.copy(xh[j][:, 4 * h:4 * h + 4, :], quads_of(XT0 + h)).then_inc(e_xh, 1)

                def act_high(j, X):
                    act.wait_ge(e_t, X + 1)
                    act.copy(ah[j][:], PS[:, AT0[j], 0:F].rearrange("p (c m) -> p c m", c=FC)).then_inc(e_ah, 1)

                def results(j, G):
                    if not (isinstance(G, int) and G == 0):
                        act.wait_ge(e_o[j], G * 8)
                    for h in range(2):
                        act.wait_ge(e_y, (G + j) * 2 + h + 1)
                        act.copy(yb[j][:, h * HALF:(h + 1) * HALF], PS[:, Y0 + h, :]).then_inc(e_ye, 1)

                def step(j, G, down_split, gate_up_split):
                    down_split()
                    act_high(j, G + j)
                    x_high(j, G + (j + 2))
                    gate_up_split()
                    sigmoid(1 - j, G + (j + 1))
                    results(j, G)

                def nothing():
                    pass

                act.wait_ge(e_gu[0], 32)
                gate_up(0, 0)
                x_high(0, 0)
                x_high(1, 1)
                act.wait_ge(e_dn[0], 16)
                down(0, 0)
                sigmoid(0, 0)
                for X in range(2):
                    step(X, 0, nothing, nothing)
                with act.Fori(2, SHB - 3, 2) as G:
                    for j in range(2):
                        step(j, G, nothing, nothing)
                act.wait_ge(e_rg, 1)
                step(0, SHB - 2, nothing, lambda: gate_up(1, 1))
                act.wait_ge(e_rd, 1)
                step(1, SHB - 2, lambda: down(1, 1), lambda: new_gate_up(1))
                with act.Fori(0, n_blocks(act), 2) as b:
                    for j in range(2):
                        step(j, b + SHB, lambda: new_down(b + (j + 1)), lambda: new_gate_up(b + (j + 2)))

            @block.vector
            def _(v):
                gate_up, down, new_gate_up, new_down = split_engine(v, False)

                def gated(j, X, b):
                    v.wait_ge(e_s, X + 1)
                    w = 1.0 if b is None else wtab[:, bass.ds(b, 1)]
                    v.scalar_tensor_tensor(ga[j][:], PS[:, GU0 + j, 0:F], w, sg[j][:], ALU.mult, ALU.mult).then_inc(e_w, 1)
                    v.wait_ge(e_w, X + 1)
                    v.tensor_tensor(ga[j][:], ga[j][:], PS[:, GU0 + j, F:2 * F], ALU.mult).then_inc(e_a, 1)

                def x_low(j, X):
                    for h in range(2):
                        v.wait_ge(e_xh, X * 2 + h + 1)
                        v.tensor_tensor(xl[j][:, 4 * h:4 * h + 4, :], quads_of(XT0 + h), xh[j][:, 4 * h:4 * h + 4, :].bitcast(F32),
                                        ALU.subtract).then_inc(e_xl, 1)

                def act_low(j, X):
                    v.wait_ge(e_ah, X + 1)
                    v.tensor_tensor(al[j][:], PS[:, AT0[j], 0:F].rearrange("p (c m) -> p c m", c=FC), ah[j][:].bitcast(F32),
                                    ALU.subtract).then_inc(e_al, 1)

                def step(j, G, next_b, down_split, gate_up_split):
                    down_split()
                    act_low(j, G + j)
                    x_low(j, G + (j + 2))
                    gate_up_split()
                    gated(1 - j, G + (j + 1), next_b)

                def nothing():
                    pass

                gate_up(0, 0)
                x_low(0, 0)
                x_low(1, 1)
                down(0, 0)
                gated(0, 0, None)
                for X in range(2):
                    step(X, 0, None, nothing, nothing)
                with v.Fori(2, SHB - 3, 2) as G:
                    for j in range(2):
                        step(j, G, None, nothing, nothing)
                step(0, SHB - 2, None, nothing, lambda: gate_up(1, 1))
                step(1, SHB - 2, 0, lambda: down(1, 1), lambda: new_gate_up(1))
                with v.Fori(0, n_blocks(v), 2) as b:
                    for j in range(2):
                        step(j, b + SHB, b + (j + 1), lambda: new_down(b + (j + 1)), lambda: new_gate_up(b + (j + 2)))

            @block.tensor
            def _(pe):
                def gate_up(j, X, half, rank, slot):
                    if half == 0:
                        pe.wait_ge(e_xl, X * 2 + 2)
                    pe.wait_ge(e_lgu, rank * GU_PARTS + (GU_PARTS // 2) * (half + 1))
                    for dc in range(half * DC // 2, (half + 1) * DC // 2):
                        for k, (xp, wp) in enumerate(((xh, eh), (xl, eh), (xh, el))):
                            if isinstance(slot, int):
                                w = wp[:, slot, 0:2, dc * F:(dc + 1) * F]
                            else:
                                w = wp[:, bass.ds(slot, 1), 0:2, dc * F:(dc + 1) * F].rearrange("p s k n -> p (s k) n")
                            mm = pe.matmul(PS[:, GU0 + j, :], xp[j][:, dc, :], w, start=(dc == 0 and k == 0), stop=(dc == DC - 1 and k == 2))
                    if half:
                        mm.then_inc(e_p, 1)

                def x_transposed(j, gathered):
                    pe.wait_ge(e_g[j], gathered)
                    rows = xg[j][:].rearrange("p (m c) -> p c m", c=DC)
                    for h in range(2):
                        for q in range(4):
                            mm = pe.transpose(PS[:, XT0 + h, q * P:(q + 1) * P], rows[:, 4 * h + q, :], ident[:])
                        mm.then_inc(e_x, 1)

                def act_transposed(j, X):
                    pe.wait_ge(e_a, X + 1)
                    cols = ga[j][:].rearrange("p (m c) -> p c m", c=FC)
                    for fc in range(FC):
                        mm = pe.transpose(PS[:, AT0[j], fc * P:(fc + 1) * P], cols[:, fc, :], ident[:])
                    mm.then_inc(e_t, 1)

                def down(j, X, rank, slot):
                    pe.wait_ge(e_al, X + 1)
                    pe.wait_ge(e_ld, (rank + 1) * DN_PARTS)
                    if not (isinstance(X, int) and X == 0):
                        pe.wait_ge(e_ye, X * 2)
                    for h in range(2):
                        n = 0
                        for fc in range(FC):
                            for ap, wp in ((ah, eh), (al, eh), (ah, el)):
                                c0 = fc * D + h * HALF
                                if isinstance(slot, int):
                                    w = wp[:, slot, 2, c0:c0 + HALF]
                                else:
                                    w = wp[:, bass.ds(slot, 1), 2, c0:c0 + HALF].rearrange("p s n -> p (s n)")
                                mm = pe.matmul(PS[:, Y0 + h, :], ap[j][:, fc, :], w, start=(n == 0), stop=(n == 3 * FC - 1))
                                n += 1
                        mm.then_inc(e_y, 1)

                def step(j, G, now, ahead):
                    gate_up(1 - j, G + (j + 1), 0, *ahead)
                    act_transposed(j, G + j)
                    x_transposed(j, G * 8 + 32)
                    gate_up(1 - j, G + (j + 1), 1, *ahead)
                    down(j, G + j, *now)

                def routed(b):
                    return entry(pe, 0, b, N_EXPERTS), entry(pe, 2, b, 1)

                x_transposed(0, 16)
                pe.wait_ge(e_xl, 2)
                x_transposed(1, 16)
                for half in range(2):
                    gate_up(0, 0, half, 0, 0)
                for X in range(2):
                    step(X, 0, (0, 0), (0, 0))
                with pe.Fori(2, SHB - 3, 2) as G:
                    for j in range(2):
                        step(j, G, (0, 0), (0, 0))
                step(0, SHB - 2, (0, 0), (0, 0))
                step(1, SHB - 2, (0, 0), (1, 1))
                with pe.Fori(0, n_blocks(pe), 2) as b:
                    blocks = [routed(b + i) for i in range(3)]
                    for j in range(2):
                        step(j, b + SHB, blocks[j], blocks[j + 1])

        ff = at("ff", AT, [P, NT, D], F32)
        xf = at("xf", AT + 32, [P, NT, D], F32)
        of = at("of", AT + 64, [P, NT, D], F32)
        rowg = at("rowg", AT + 96, [P, D], F32)
        diagf = at("diagf", AT + 100, [P, DC, P], F32)
        fj = at("fj", AT + 104, [P, D], F32)
        f_l = s_x
        f_x = sem("f_x")
        f_q = sem("f_q")
        f_r = sem("f_r")
        f_v = sem("f_v")
        f_d = sem("f_d")
        f_b = sem("f_b")
        f_g = sem("f_g")
        f_m = sem("f_m")
        f_o = sem("f_o")
        f_s = sem("f_s")

        with nc.Block() as block:
            @block.sync
            def _(sp):
                for t in range(NT):
                    sp.dma_start(ff[:, t, :], acc_dram[t * P:(t + 1) * P, :]).then_inc(f_l[t], 16)
                for t in range(NT):
                    sp.wait_ge(f_o, t + 1)
                    sp.dma_start(out[0, t * P:(t + 1) * P, :], of[:, t, :]).then_inc(f_s, 16)
                sp.wait_ge(f_s, 16 * NT)

            @block.gpsimd
            def _(po):
                for t in range(NT):
                    po.wait_ge(f_m, t + 1)
                    po.wait_ge(f_x, 16 * NT)
                    po.tensor_tensor(of[:, t, :], of[:, t, :], xf[:, t, :], ALU.add).then_inc(f_o, 1)

            @block.scalar
            def _(act):
                for t in range(NT):
                    act.dma_start(xf[:, t, :], x1_dram[t * P:(t + 1) * P, :]).then_inc(f_x, 16)
                for t in range(NT):
                    act.wait_ge(f_l[t], 32)
                    act.activation(fj[:], ff[:, t, :], ACT.Square, accum_out=ssum[:, 32 + t:33 + t]).then_inc(f_q, 1)
                    act.wait_ge(f_q, t + 1)
                    act.activation(root[:, 40 + t:41 + t], ssum[:, 32 + t:33 + t], ACT.Sqrt, bias=epsc[:, 0:1], scale=1.0 / D).then_inc(f_r, 1)

            @block.vector
            def _(v):
                v.tensor_tensor(diagf[:], ident[:, None, :].broadcast_to([P, DC, P]),
                                vecc[:, 3, :][:, :, None].broadcast_to([P, DC, P]), ALU.mult).then_inc(f_d, 1)
                v.wait_ge(f_b, 1)
                v.tensor_copy(rowg[:], flat2(0)).then_inc(f_g, 1)
                v.wait_ge(f_g, 1)
                for t in range(NT):
                    v.wait_ge(f_r, t + 1)
                    v.reciprocal(rstd[:, 40 + t:41 + t], root[:, 40 + t:41 + t]).then_inc(f_v, 1)
                    v.wait_ge(f_v, t + 1)
                    v.scalar_tensor_tensor(of[:, t, :], ff[:, t, :], rstd[:, 40 + t:41 + t], rowg[:], ALU.mult, ALU.mult).then_inc(f_m, 1)

            @block.tensor
            def _(pe):
                pe.wait_ge(f_d, 1)
                for h in range(2):
                    mm = pe.matmul(PS[:, h, :], ones[:], diagf[:, 4 * h:4 * h + 4, :], start=True, stop=True)
                mm.then_inc(f_b, 1)


_INS = ['x', 'c', 'w_ada', 'b_ada', 'g_pre_mix', 'g_post_mix', 'g_pre_ffn', 'g_post_ffn', 'w_in', 'b_forget',
        'w_pool', 'pool_scale', 'g_pool_out', 'g_attn_out', 'w_out', 'w_router', 'router_bias',
        'w_gate', 'w_up', 'w_down', 'ws_gate', 'ws_up', 'ws_down']


def kernel(**inputs):
    import numpy as np
    import concourse.bacc as bacc
    from concourse.bass_utils import run_bass_kernel_spmd

    nc = bacc.Bacc("TRN2", target_bir_lowering=False, num_devices=1)
    arrays, args = {}, []
    for name in _INS:
        a = np.ascontiguousarray(inputs[name])
        arrays[f"in_{name}"] = a
        args.append(nc.dram_tensor(f"in_{name}", a.shape, mybir.dt.from_np(a.dtype), kind="ExternalInput").ap())
    args.append(nc.dram_tensor("out_0", (1, T, D), F32, kind="ExternalOutput").ap())
    args.append(nc.dram_tensor("x1_dram", (T, D), F32, kind="Internal").ap())
    args.append(nc.dram_tensor("h2_dram", (T, D), F32, kind="Internal").ap())
    args.append(nc.dram_tensor("acc_dram", (T + P, D), F32, kind="Internal").ap())
    build(nc, *args)
    r = run_bass_kernel_spmd(nc, [arrays], core_ids=[0])
    return r.results[0]["out_0"]
```
